# Optimizing a Trainium2 kernel written in Bass

```python
import math
import jax, jax.numpy as jnp
from jax import lax
import numpy as np

D_MODEL = 1024
BATCH = 1
SEQ = 128
DEPTH = 2
DEC_BATCH = 1
DEC_SEQ = 256
PAST_LEN = 128

GRID_W = 64
N_EVEN = (DEPTH + 1) // 2
N_ODD = DEPTH // 2
N_MOD = 6
EPS = 1e-6

SSD_HEADDIM = 64
SSD_HEADS = D_MODEL // SSD_HEADDIM
D_SSD = SSD_HEADS * SSD_HEADDIM
SSD_GROUPS = 4
SSD_STATE = 128
SSD_CHUNK = 128
CONV_W = 5
CONV_CH = D_SSD + 2 * SSD_GROUPS * SSD_STATE
D_SGU = D_MODEL
SGU_GROUPS = 4
SGU_GDIM = D_SGU // SGU_GROUPS
SGU_CHUNK = 128
IN_COLS = D_SSD + CONV_CH + 2 * SSD_HEADS + 2 * D_SGU
MLA_HEADS = 8
Q_RANK = 384
KV_RANK = 256
QK_NOPE = 128
QK_ROPE = 64
V_HEAD = 128
QK_DIM = QK_NOPE + QK_ROPE
ROPE_AXIS = QK_ROPE // 2
ROPE_THETA = 10000.0
Q_BLOCK = 128
D_FF = 2816
N_EXPERTS = 8
TOP_K = 2
MOE_BLOCK = 128

kernel_name = 'hybrid_ssd_sgu_mla_dit_step'

def rms_norm(x):
    xf = x.astype(jnp.float32)
    return (xf * lax.rsqrt(jnp.mean(xf * xf, axis=-1, keepdims=True) + EPS)).astype(x.dtype)

def modulate(x, shift, scale):
    return rms_norm(x) * (1 + scale) + shift

def decay_matrix(cs):
    t = cs.shape[-1]
    lower = jnp.tril(jnp.ones((t, t), dtype=bool))
    return jnp.exp(jnp.where(lower, cs[..., :, None] - cs[..., None, :], -jnp.inf))

def ssd_scan(x, dt, a, bm, cm, init_state):
    f32 = jnp.float32
    b, l, h, p = x.shape
    nc = l // SSD_CHUNK
    hpg = h // SSD_GROUPS
    xc = (x.astype(f32) * dt[..., None]).reshape(b, nc, SSD_CHUNK, h, p)
    ac = jnp.moveaxis((dt * a).reshape(b, nc, SSD_CHUNK, h), 3, 1)
    a_cs = jnp.cumsum(ac, axis=-1)
    bc = bm.astype(f32).reshape(b, nc, SSD_CHUNK, SSD_GROUPS, SSD_STATE)
    cc = cm.astype(f32).reshape(b, nc, SSD_CHUNK, SSD_GROUPS, SSD_STATE)
    cb = jnp.repeat(jnp.einsum('bclgn,bcsgn->bcgls', cc, bc), hpg, axis=2)
    y_diag = jnp.einsum('bchls,bhcls,bcshp->bclhp', cb, decay_matrix(a_cs), xc)
    b_h = jnp.repeat(bc, hpg, axis=3)
    c_h = jnp.repeat(cc, hpg, axis=3)
    decay_to_end = jnp.exp(a_cs[..., -1:] - a_cs)
    chunk_states = jnp.einsum('bclhn,bhcl,bclhp->bchpn', b_h, decay_to_end, xc)
    chunk_states = jnp.concatenate([init_state.astype(f32)[:, None], chunk_states], axis=1)
    chunk_cs = jnp.cumsum(jnp.pad(a_cs[..., -1], ((0, 0), (0, 0), (1, 0))), axis=-1)
    states = jnp.einsum('bhzc,bchpn->bzhpn', decay_matrix(chunk_cs), chunk_states)
    y_off = jnp.einsum('bclhn,bchpn,bhcl->bclhp', c_h, states[:, :-1], jnp.exp(a_cs))
    y = (y_diag + y_off).reshape(b, l, h, p).astype(x.dtype)
    return y, states[:, -1].astype(init_state.dtype)

def centred_dwconv(x, w, bias):
    k = w.shape[0]
    pad = k // 2
    l = x.shape[1]
    xp = jnp.pad(x, ((0, 0), (pad, pad), (0, 0)))
    return sum(xp[:, i:i + l] * w[i] for i in range(k)) + bias

def spatial_gating(u, v, sgu_norm, w_sp, b_sp):
    b, l, _ = v.shape
    nc = l // SGU_CHUNK
    vb = (rms_norm(v) * sgu_norm).reshape(b, nc, SGU_CHUNK, SGU_GROUPS, SGU_GDIM)
    sv = jnp.einsum('gts,bcsgd->bctgd', w_sp, vb) + b_sp.T[:, :, None]
    return u * sv.reshape(b, l, D_SGU)

def ssd_sgu_mixer(h, init_state, w_in, conv_w, conv_b, dt_bias, a_log, d_skip, ssd_norm,
                  sgu_norm, w_sp, b_sp, w_out):
    b, l, _ = h.shape
    i1 = D_SSD
    i2 = i1 + CONV_CH
    i3 = i2 + 2 * SSD_HEADS
    i4 = i3 + D_SGU
    z, xbc, dt_raw, u, v = jnp.split(h @ w_in, [i1, i2, i3, i4], axis=-1)
    xbc = jax.nn.silu(centred_dwconv(xbc, conv_w, conv_b))
    xs, bm, cm = jnp.split(xbc, [D_SSD, D_SSD + SSD_GROUPS * SSD_STATE], axis=-1)
    xs = xs.reshape(b, l, SSD_HEADS, SSD_HEADDIM)
    bm = bm.reshape(b, l, SSD_GROUPS, SSD_STATE)
    cm = cm.reshape(b, l, SSD_GROUPS, SSD_STATE)
    dt = jax.nn.softplus(dt_raw.astype(jnp.float32).reshape(b, l, 2, SSD_HEADS) + dt_bias.astype(jnp.float32))
    a = -jnp.exp(a_log.astype(jnp.float32))
    y_f, s_f = ssd_scan(xs, dt[:, :, 0], a[0], bm, cm, init_state[:, 0])
    y_b, s_b = ssd_scan(xs[:, ::-1], dt[:, ::-1, 1], a[1], bm[:, ::-1], cm[:, ::-1], init_state[:, 1])
    y = y_f + y_b[:, ::-1] + xs * d_skip[:, None]
    y = rms_norm(y.reshape(b, l, D_SSD) * jax.nn.silu(z)) * ssd_norm
    y_sgu = spatial_gating(u, v, sgu_norm, w_sp, b_sp)
    out = jnp.concatenate([y, y_sgu], axis=-1) @ w_out
    return out, jnp.stack([s_f, s_b], axis=1)

def rope_rotate(x, ang):
    m = ang.shape[-1]
    cos = jnp.cos(ang)[:, None, :].astype(x.dtype)
    sin = jnp.sin(ang)[:, None, :].astype(x.dtype)
    x1, x2 = x[..., :m], x[..., m:]
    return jnp.concatenate([x1 * cos - x2 * sin, x1 * sin + x2 * cos], axis=-1)

def axial_rope(x):
    l = x.shape[1]
    rows = l // GRID_W
    row = jnp.repeat(jnp.arange(rows), GRID_W).astype(jnp.float32)
    col = jnp.tile(jnp.arange(GRID_W), rows).astype(jnp.float32)
    inv = ROPE_THETA ** (-jnp.arange(0, ROPE_AXIS, 2, dtype=jnp.float32) / ROPE_AXIS)
    xr = x[..., QK_NOPE:QK_NOPE + ROPE_AXIS]
    xc = x[..., QK_NOPE + ROPE_AXIS:]
    return jnp.concatenate([x[..., :QK_NOPE], rope_rotate(xr, row[:, None] * inv),
                            rope_rotate(xc, col[:, None] * inv)], axis=-1)

def mla_queries(h, w_dq, q_a_norm, w_uq, q_norm):
    b, l, _ = h.shape
    q = (rms_norm(h @ w_dq) * q_a_norm) @ w_uq
    return rms_norm(q.reshape(b, l, MLA_HEADS, QK_DIM)) * q_norm

def mla_compress_kv(h, w_dkv, kv_a_norm):
    kv_a = h @ w_dkv
    return rms_norm(kv_a[..., :KV_RANK]) * kv_a_norm, kv_a[..., KV_RANK:]

def mla_expand_kv(c_kv, k_pe, w_ukv, k_norm):
    b, l, _ = c_kv.shape
    kv = (c_kv @ w_ukv).reshape(b, l, MLA_HEADS, QK_NOPE + V_HEAD)
    k = jnp.concatenate([kv[..., :QK_NOPE],
                         jnp.broadcast_to(k_pe[:, :, None, :], (b, l, MLA_HEADS, QK_ROPE))], axis=-1)
    return rms_norm(k) * k_norm, kv[..., QK_NOPE:]

def attention(q, k, v):
    b, lq, h, dh = q.shape
    nb = lq // Q_BLOCK
    qb = jnp.moveaxis(q.reshape(b, nb, Q_BLOCK, h, dh), 1, 0)
    scale = dh ** -0.5

    def one_block(qi):
        s = jnp.einsum('bqhd,bkhd->bhqk', qi, k, preferred_element_type=jnp.float32) * scale
        p = jax.nn.softmax(s, axis=-1).astype(v.dtype)
        return jnp.einsum('bhqk,bkhd->bqhd', p, v)

    o = lax.map(one_block, qb)
    return jnp.moveaxis(o, 0, 1).reshape(b, lq, h, v.shape[-1])

def mla_output(o, w_o):
    b, l = o.shape[:2]
    return o.reshape(b, l, MLA_HEADS * V_HEAD) @ w_o

def swiglu(h, wg, wu, wd):
    return (jax.nn.silu(h @ wg) * (h @ wu)) @ wd

def moe_swiglu(h, w_router, wg, wu, wd):
    shp = h.shape
    t = h.reshape(-1, shp[-1])
    n_tok = t.shape[0]
    logits = jnp.einsum('td,de->te', t, w_router, preferred_element_type=jnp.float32)
    top_logit, top_e = lax.top_k(logits, TOP_K)
    gates = jax.nn.softmax(top_logit, axis=-1)
    n_assign = n_tok * TOP_K
    flat_e = top_e.reshape(-1)
    order = jnp.argsort(flat_e)
    e_sorted = flat_e[order]
    tok_sorted = order // TOP_K
    gate_sorted = gates.reshape(-1)[order]
    counts = jnp.bincount(flat_e, length=N_EXPERTS)
    padded = (counts + MOE_BLOCK - 1) // MOE_BLOCK * MOE_BLOCK
    pad_end = jnp.cumsum(padded)
    pad_start = pad_end - padded
    start = jnp.cumsum(counts) - counts
    dest = pad_start[e_sorted] + (jnp.arange(n_assign) - start[e_sorted])
    n_rows = -(-n_assign // MOE_BLOCK) * MOE_BLOCK + N_EXPERTS * MOE_BLOCK
    n_blocks = n_rows // MOE_BLOCK
    buf = jnp.zeros((n_rows, shp[-1]), t.dtype).at[dest].set(t[tok_sorted])
    block_e = jnp.minimum(jnp.searchsorted(pad_end, jnp.arange(n_blocks) * MOE_BLOCK, side='right'),
                          N_EXPERTS - 1)

    def expert_block(args):
        xb, e = args
        return (jax.nn.silu(xb @ wg[e]) * (xb @ wu[e])) @ wd[e]

    out = lax.map(expert_block, (buf.reshape(n_blocks, MOE_BLOCK, shp[-1]), block_e)).reshape(n_rows, shp[-1])
    y = jnp.zeros_like(t).at[tok_sorted].add(out[dest] * gate_sorted[:, None].astype(t.dtype))
    return y.reshape(shp)

def setup_inputs(seed: int = 0) -> dict:
    key = jax.random.key(seed)
    ks = iter(jax.random.split(key, 48))
    f32 = jnp.float32

    def nrm(shape, scale):
        return jax.random.normal(next(ks), shape, f32) * scale

    def gain(shape):
        return 1.0 + nrm(shape, 0.02)

    dt0 = jnp.exp(jax.random.uniform(next(ks), (N_EVEN, 2, SSD_HEADS), f32,
                                     minval=math.log(1e-3), maxval=math.log(1e-1)))
    dt_bias = dt0 + jnp.log(-jnp.expm1(-dt0))
    a_log = jnp.log(jax.random.uniform(next(ks), (N_EVEN, 2, SSD_HEADS), f32, minval=1.0, maxval=16.0))
    return {
        'x_prompt': nrm((BATCH, SEQ, D_MODEL), 1.0),
        'x_sample': nrm((DEC_BATCH, DEC_SEQ, D_MODEL), 1.0),
        'c': nrm((DEC_BATCH, D_MODEL), 1.0),
        'state_ssm': nrm((DEC_BATCH, N_EVEN, 2, SSD_HEADS, SSD_HEADDIM, SSD_STATE), 0.5),
        'cache_ckv': nrm((DEC_BATCH, N_ODD, PAST_LEN, KV_RANK), 1.0),
        'cache_kpe': nrm((DEC_BATCH, N_ODD, PAST_LEN, QK_ROPE), 1.0),
        'c_ctx': nrm((D_MODEL,), 1.0),
        'w_mod': nrm((DEPTH, D_MODEL, N_MOD * D_MODEL), 0.5 * D_MODEL ** -0.5),
        'b_mod': nrm((DEPTH, N_MOD * D_MODEL), 0.02),
        'w_in': nrm((N_EVEN, D_MODEL, IN_COLS), D_MODEL ** -0.5),
        'conv_w': nrm((N_EVEN, CONV_W, CONV_CH), CONV_W ** -0.5),
        'conv_b': nrm((N_EVEN, CONV_CH), 0.02),
        'dt_bias': dt_bias,
        'a_log': a_log,
        'd_skip': gain((N_EVEN, SSD_HEADS)),
        'ssd_norm': gain((N_EVEN, D_SSD)),
        'sgu_norm': gain((N_EVEN, D_SGU)),
        'w_sp': nrm((N_EVEN, SGU_GROUPS, SGU_CHUNK, SGU_CHUNK), SGU_CHUNK ** -0.5),
        'b_sp': gain((N_EVEN, SGU_GROUPS, SGU_CHUNK)),
        'w_out': nrm((N_EVEN, D_SSD + D_SGU, D_MODEL), (D_SSD + D_SGU) ** -0.5),
        'ffn_w_gate': nrm((N_EVEN, D_MODEL, D_FF), D_MODEL ** -0.5),
        'ffn_w_up': nrm((N_EVEN, D_MODEL, D_FF), D_MODEL ** -0.5),
        'ffn_w_down': nrm((N_EVEN, D_FF, D_MODEL), D_FF ** -0.5),
        'w_dq': nrm((N_ODD, D_MODEL, Q_RANK), D_MODEL ** -0.5),
        'q_a_norm': gain((N_ODD, Q_RANK)),
        'w_uq': nrm((N_ODD, Q_RANK, MLA_HEADS * QK_DIM), Q_RANK ** -0.5),
        'w_dkv': nrm((N_ODD, D_MODEL, KV_RANK + QK_ROPE), D_MODEL ** -0.5),
        'kv_a_norm': gain((N_ODD, KV_RANK)),
        'w_ukv': nrm((N_ODD, KV_RANK, MLA_HEADS * (QK_NOPE + V_HEAD)), KV_RANK ** -0.5),
        'q_norm': gain((N_ODD, QK_DIM)),
        'k_norm': gain((N_ODD, QK_DIM)),
        'w_o': nrm((N_ODD, MLA_HEADS * V_HEAD, D_MODEL), (MLA_HEADS * V_HEAD) ** -0.5),
        'router': nrm((N_ODD, D_MODEL, N_EXPERTS), D_MODEL ** -0.5),
        'moe_w_gate': nrm((N_ODD, N_EXPERTS, D_MODEL, D_FF), D_MODEL ** -0.5),
        'moe_w_up': nrm((N_ODD, N_EXPERTS, D_MODEL, D_FF), D_MODEL ** -0.5),
        'moe_w_down': nrm((N_ODD, N_EXPERTS, D_FF, D_MODEL), D_FF ** -0.5),
    }

def reference(x_prompt, x_sample, c, state_ssm, cache_ckv, cache_kpe, c_ctx, w_mod, b_mod,
              w_in, conv_w, conv_b, dt_bias, a_log, d_skip, ssd_norm, sgu_norm, w_sp, b_sp, w_out,
              ffn_w_gate, ffn_w_up, ffn_w_down,
              w_dq, q_a_norm, w_uq, w_dkv, kv_a_norm, w_ukv, q_norm, k_norm, w_o,
              router, moe_w_gate, moe_w_up, moe_w_down):
    xp, xs = x_prompt, x_sample
    silu_ctx = jax.nn.silu(c_ctx)
    silu_c = jax.nn.silu(c)
    new_ssm, new_ckv, new_kpe = [], [], []
    for i in range(DEPTH):
        j = i // 2
        mp = jnp.split(silu_ctx @ w_mod[i] + b_mod[i], N_MOD, axis=-1)
        ms = jnp.split((silu_c @ w_mod[i] + b_mod[i])[:, None, :], N_MOD, axis=-1)
        hp = modulate(xp, mp[0], mp[1])
        hs = modulate(xs, ms[0], ms[1])
        if i % 2 == 0:
            mix = (w_in[j], conv_w[j], conv_b[j], dt_bias[j], a_log[j], d_skip[j], ssd_norm[j],
                   sgu_norm[j], w_sp[j], b_sp[j], w_out[j])
            zero_state = jnp.zeros((xp.shape[0], 2, SSD_HEADS, SSD_HEADDIM, SSD_STATE), xp.dtype)
            op, ctx_state = ssd_sgu_mixer(hp, zero_state, *mix)
            os_, _ = ssd_sgu_mixer(hs, state_ssm[:, j], *mix)
            new_ssm.append(ctx_state)
        else:
            qp = mla_queries(hp, w_dq[j], q_a_norm[j], w_uq[j], q_norm[j])
            ckv_p, kpe_p = mla_compress_kv(hp, w_dkv[j], kv_a_norm[j])
            kp, vp = mla_expand_kv(ckv_p, kpe_p, w_ukv[j], k_norm[j])
            op = mla_output(attention(qp, kp, vp), w_o[j])
            new_ckv.append(ckv_p)
            new_kpe.append(kpe_p)
            qs = axial_rope(mla_queries(hs, w_dq[j], q_a_norm[j], w_uq[j], q_norm[j]))
            ckv_s, kpe_s = mla_compress_kv(hs, w_dkv[j], kv_a_norm[j])
            ks_, vs_ = mla_expand_kv(ckv_s, kpe_s, w_ukv[j], k_norm[j])
            kc, vc = mla_expand_kv(cache_ckv[:, j], cache_kpe[:, j], w_ukv[j], k_norm[j])
            os_ = mla_output(attention(qs, jnp.concatenate([kc, axial_rope(ks_)], axis=1),
                                       jnp.concatenate([vc, vs_], axis=1)), w_o[j])
        xp = xp + mp[2] * op
        xs = xs + ms[2] * os_
        hp = modulate(xp, mp[3], mp[4])
        hs = modulate(xs, ms[3], ms[4])
        if i % 2 == 0:
            fp = swiglu(hp, ffn_w_gate[j], ffn_w_up[j], ffn_w_down[j])
            fs = swiglu(hs, ffn_w_gate[j], ffn_w_up[j], ffn_w_down[j])
        else:
            fp = moe_swiglu(hp, router[j], moe_w_gate[j], moe_w_up[j], moe_w_down[j])
            fs = moe_swiglu(hs, router[j], moe_w_gate[j], moe_w_up[j], moe_w_down[j])
        xp = xp + mp[5] * fp
        xs = xs + ms[5] * fs
    new_state_ssm = jnp.stack(new_ssm, axis=1)
    new_cache_ckv = jnp.stack(new_ckv, axis=1)
    new_cache_kpe = jnp.stack(new_kpe, axis=1)
    return (xp, xs, new_state_ssm, new_cache_ckv, new_cache_kpe)


_drawn_inputs = setup_inputs


def setup_inputs(seed=0):
    import zlib

    import numpy as np

    out = dict(_drawn_inputs(seed))
    spreads = {}
    factors = {'cache_ckv': 2.901,
     'cache_kpe': 6.518,
     'd_skip': 8.0,
     'ssd_norm': 8.0,
     'sgu_norm': 8.0,
     'b_sp': 8.0,
     'q_a_norm': 8.0,
     'kv_a_norm': 2.783,
     'q_norm': 8.0,
     'k_norm': 8.0}
    for name, (base, spread) in spreads.items():
        noise = np.random.default_rng([zlib.crc32(name.encode()), seed]).standard_normal(out[name].shape)
        drawn = base * np.exp(spread * noise) if base else spread * noise
        out[name] = __import__('jax').numpy.asarray(drawn.astype(out[name].dtype))
    for name, factor in factors.items():
        out[name] = (out[name] * factor).astype(out[name].dtype)
    return out
```

```python
from contextlib import ExitStack

import numpy as np
import concourse.bass as bass
from concourse import mybir

F32 = mybir.dt.float32
I32 = mybir.dt.int32
U32 = mybir.dt.uint32
ACT = mybir.ActivationFunctionType
ALU = mybir.AluOpType
AXX = mybir.AxisListType.X

P = 128
D = 1024
KT = D // P
NT = 3
TOK = NT * P
LAT = 2 * P
EPS = 1e-6
NMOD = 6 * KT
HEADS, HD, GROUPS, STATE = 16, 64, 4, 128
HPG = HEADS // GROUPS
CCT = 16
CW = 5
PAD = CW // 2
RAW = PAD + P + PAD + LAT + PAD
CVW = RAW - 2 * PAD
TOK0 = [0, P + PAD, 2 * P + PAD]
SGRP, SGD = 4, 256
MH, QR, KVR, NOPE, ROPE, VH = 8, 384, 256, 128, 64, 128
QK = NOPE + ROPE
KTILES = 4
FF = 2816
FT = FF // P
NE = 8
GRID_W = 64
RING = 4
SLOT = 4096
BANKS = 8
NEG = -1e30
WIDTHS = [64, 96, 128, 192, 256, 384]
GU = [(2 * j, 2) for j in range(10)] + [(20, 1), (21, 1)]
DN = [(dp, fh) for dp in range(4) for fh in range(2)]
FH = FT // 2


def constants():
    i = np.arange(P)
    upper = (i[:, None] <= i[None, :]).astype(np.float32)
    lower = (i[:, None] >= i[None, :]).astype(np.float32)
    eye = np.eye(P, dtype=np.float32)
    inv = (np.float32(10000.0) ** (-np.arange(0, ROPE // 2, 2, dtype=np.float32) / np.float32(ROPE // 2))).astype(np.float32)
    tabs = []
    for tile in range(2):
        tok = tile * P + i
        ang = np.stack([(tok // GRID_W).astype(np.float32)[:, None] * inv,
                        (tok % GRID_W).astype(np.float32)[:, None] * inv], axis=1)
        tabs += [np.cos(ang).reshape(P, 32), np.sin(ang).reshape(P, 32)]
    return np.concatenate([eye, upper, lower, np.ones((P, P), np.float32),
                           np.where(upper > 0, 0.0, NEG), np.where(lower > 0, 0.0, NEG), upper - eye]
                          + tabs, axis=1).astype(np.float32)


def hybrid_trunk(nc, x_prompt, x_sample, c, state_ssm, cache_ckv, cache_kpe, c_ctx, w_mod, b_mod,
                 w_in, conv_w, conv_b, dt_bias, a_log, d_skip, ssd_norm, sgu_norm, w_sp, b_sp, w_out,
                 ffn_w_gate, ffn_w_up, ffn_w_down, w_dq, q_a_norm, w_uq, w_dkv, kv_a_norm, w_ukv,
                 q_norm, k_norm, w_o, router, moe_w_gate, moe_w_up, moe_w_down,
                 y_prompt, y_sample, new_state, new_ckv, new_kpe):
    ctx = ExitStack()
    with ctx:
        def sb(name, shape, dt=F32):
            return ctx.enter_context(nc.sbuf_tensor(name, shape, dt))

        def sem(name):
            return ctx.enter_context(nc.semaphore(name))

        ring = sb("ring", [P, RING, SLOT])
        X = sb("X", [P, NT, D])
        HTXN = sb("HTXN", [P, 2 * KT * TOK])
        HT = HTXN[:, 0:KT * TOK].rearrange("p (k t) -> p k t", k=KT)
        XN = HTXN[:, KT * TOK:].rearrange("p (t d) -> p t d", t=NT)
        consts_np = constants()
        CST = sb("CST", [P, consts_np.shape[1]])
        ident, upper, lower, ones = (CST[:, n * P:(n + 1) * P] for n in range(4))
        mask = [CST[:, 4 * P:5 * P], CST[:, 5 * P:6 * P]]
        before = CST[:, 6 * P:7 * P]
        cosT = [CST[:, 7 * P + 64 * i:7 * P + 64 * i + 32].rearrange("p (a m) -> p a m", a=2) for i in range(2)]
        sinT = [CST[:, 7 * P + 64 * i + 32:7 * P + 64 * i + 64].rearrange("p (a m) -> p a m", a=2) for i in range(2)]
        tri = [upper, lower]
        colT = sb("colT", [P, 2, 112])
        modT = sb("modT", [P, 2, NMOD, 2])
        GB = sb("GB", [P, 2, D])
        rows = sb("rows", [P, 32 + 32 + 16 + 2 * QK + KVR])
        dtb_r, alog_r, dsk_r = rows[:, 0:32], rows[:, 32:64], rows[:, 64:80]
        qn_r, kn_r, kvn_r = rows[:, 80:80 + QK], rows[:, 80 + QK:80 + 2 * QK], rows[:, 80 + 2 * QK:]
        wdt = sb("wdt", [P, KT, 32])
        wrt = sb("wrt", [P, KT, NE])
        wspT = sb("wspT", [P, SGRP, P])
        stat = sb("stat", [P, 256])
        sv = sb("sv", [P, 2, KT])
        bmodc = colT[:, 0, 16:112].rearrange("p (l m) -> p l m", l=2)
        convw = colT[:, 1, 0:80].rearrange("p (i c) -> p i c", i=CW)
        convb, ssdn, bspc, qanc = colT[:, 1, 80:96], colT[:, 1, 96:104], colT[:, 1, 104:108], colT[:, 1, 108:111]

        ARENA = 22100
        arena = sb("arena", [P, ARENA])

        def lay(sizes):
            out, at = [], 0
            for n in sizes:
                out.append(arena[:, at:at + n])
                at += n
            assert at <= ARENA, at
            return out

        cv_a, raw_a, z_a, u_a, v_a, bt_a, w_a, sgn_r = lay([CCT * CVW, 4 * RAW, NT * D, NT * D, NT * D, NT * 512, 2048, D])
        CV = cv_a.rearrange("p (c t) -> p c t", c=CCT)
        raw = raw_a.rearrange("p (b t) -> p b t", b=4)
        cb = raw_a[:, 0:NT * 512].rearrange("p (c g l) -> p c g l", c=NT, g=GROUPS)
        Z, U, V = (a.rearrange("p (t d) -> p t d", t=NT) for a in (z_a, u_a, v_a))
        XS = V
        BT = bt_a.rearrange("p (t n) -> p t n", t=NT)
        W = w_a.rearrange("p (b n) -> p b n", b=2)
        praw = w_a[:, 0:6 * P].rearrange("p (r n) -> p r n", r=6)
        st_raw = w_a.rearrange("p (d i n) -> p d i n", d=2, i=KT)
        stT = GB
        xdt = HTXN[:, 0:6 * D].rearrange("p (c d n) -> p c d n", c=NT, d=2)
        cst = cv_a[:, 0:2048].rearrange("p (d i n) -> p d i n", d=2, i=KT)
        off = cv_a[:, 2048:3072].rearrange("p (b n) -> p b n", b=2)
        YT = cv_a[:, 0:2 * KT * TOK].rearrange("p (k t) -> p k t", k=2 * KT)
        aT_a, sg_a, tmp_a = lay([FT * TOK, 2 * TOK, 1024])
        aT = aT_a.rearrange("p (f t) -> p f t", f=FT)
        sg = sg_a.rearrange("p (b t) -> p b t", b=2)
        ftmp = tmp_a.rearrange("p (b n) -> p b n", b=2)
        (v4_a, kt_a, kp_a, qt_a, qp_a, kq_a, ckvT_a, ckv_a, kpe_a, qaT_a) = lay(
            [KTILES * D, MH * 512, 4 * 512, MH * TOK, 4 * TOK, 2 * MH * QK, 2 * 512, KTILES * KVR, KTILES * ROPE, 3 * TOK])
        VV = v4_a.rearrange("p (k n) -> p k n", k=KTILES)
        kTn = kt_a.rearrange("p (h t) -> p h t", h=MH)
        kTr = kp_a.rearrange("p (h t) -> p h t", h=4)
        qTn = qt_a.rearrange("p (h t) -> p h t", h=MH)
        qTr = qp_a.rearrange("p (h t) -> p h t", h=4)
        kq_v = kq_a.rearrange("p (b n) -> p b n", b=2)
        KQN = kq_v[:, :, 0:D].rearrange("p b (h n) -> p b h n", h=MH)
        KQR = kq_v[:, :, D:].rearrange("p b (h n) -> p b h n", h=MH)
        ckvT = ckvT_a.rearrange("p (k t) -> p k t", k=2)
        ckv = ckv_a.rearrange("p (k n) -> p k n", k=KTILES)
        kpe = kpe_a.rearrange("p (k n) -> p k n", k=KTILES)
        qaT = qaT_a.rearrange("p (k t) -> p k t", k=3)
        xn_a = HTXN[:, KT * TOK:]
        qa = xn_a[:, 0:3 * QR].rearrange("p (t n) -> p t n", t=NT)
        junk = xn_a[:, 1152:1152 + MH * QK]
        rt = xn_a[:, 1152:1152 + 1024].rearrange("p (b h a m) -> p b h a m", b=4, h=MH, a=2)
        PR = xn_a[:, 0:2 * TOK].rearrange("p (b n) -> p b n", b=2)
        PT = xn_a[:, 768:768 + 2 * 896].rearrange("p (b n) -> p b n", b=2)
        OT = HT
        (_, _, _, yT_a, yt_a, pg_a, pgT_a, yac_a) = lay(
            [FT * TOK, 2 * TOK, 1024, KT * TOK, NT * D, NT * TOK, NT * TOK, NT * D])
        H2 = XN
        xeT = HT
        yT = yT_a.rearrange("p (k t) -> p k t", k=KT)
        yt = yt_a.rearrange("p (s d) -> p s d", s=NT)
        PG = pg_a.rearrange("p (t s) -> p t s", t=NT)
        PGT = pgT_a.rearrange("p (s t) -> p s t", s=NT)
        YA = yac_a.rearrange("p (t d) -> p t d", t=NT)
        gb_a = GB[:, :, :].rearrange("p s d -> p (s d)")
        PS = gb_a[:, 0:NT * TOK].rearrange("p (t s) -> p t s", t=NT)
        iota = gb_a[:, 1152:1152 + TOK]
        small = sb("small", [P, 8 * 96])
        dtx, dtu, dtw, dtv, dtA, csn, tot, ecs = (small[:, 96 * n:96 * (n + 1)] for n in range(8))
        den = dtw
        etot = dtv
        small2 = sb("small2", [P, 32 + 96])
        aexp, dtt = small2[:, 0:32], small2[:, 32:128]
        lg = small[:, 0:24].rearrange("p (t e) -> p t e", t=NT)
        top = small[:, 24:48].rearrange("p (t e) -> p t e", t=NT)
        idxf = small[:, 48:72].rearrange("p (t e) -> p t e", t=NT)
        oh1 = small[:, 96:120].rearrange("p (t e) -> p t e", t=NT)
        sel = small[:, 120:144].rearrange("p (t e) -> p t e", t=NT)
        rank = small[:, 144:171].rearrange("p (t e) -> p t e", t=NT)
        gate = small[:, 176:203].rearrange("p (t e) -> p t e", t=NT)
        gpair = small[:, 208:220]
        cnt = small[:, 224:232]
        vsum = small[:, 232:242]
        e8 = small[:, 244:252]
        idxu = sb("idxu", [P, NT, 8], U32)
        vtab = sb("vtab", [P, 2, 10], I32)
        nmx, psum_ = stat[:, 200:224], stat[:, 224:248]

        PSUM = [ctx.enter_context(nc.psum_tensor(f"bank{b}", [P, 512], F32)) for b in range(BANKS)]

        def sems(*names):
            return [sem(n) for n in names]

        ring_full = [sem(f"ring_full{s}") for s in range(RING)]
        bank_full = [sem(f"bank_full{b}") for b in range(BANKS)]
        bank_free = [sem(f"bank_free{b}") for b in range(BANKS)]
        chunk_used, w_used = sems("chunk_used", "w_used")
        x_loaded, const_loaded, small_loaded, prow_loaded, wsp_loaded, st_loaded, cache_loaded, iota_loaded = sems(
            "x_loaded", "const_loaded", "small_loaded", "prow_loaded", "wsp_loaded", "st_loaded", "cache_loaded", "iota_loaded")
        down_begun = sem("down_begun")
        state_out, kv_out, y_out = sems("state_out", "kv_out", "y_out")
        dve_step, pool_step = sems("dve_step", "pool_step")
        sq_done, ms_ready, rt_ready = sems("sq_done", "ms_ready", "rt_ready")
        xn_ready, x_updated, mod_ready, sv_ready = sems("xn_ready", "x_updated", "mod_ready", "sv_ready")
        raw_zero, conv_done, cv_ready, vn_ready = sems("raw_zero", "conv_done", "cv_ready", "vn_ready")
        dt_arg, dt_exp, dt_w, dt_ln, dt_ready, dta_ready = sems("dt_arg", "dt_exp", "dt_w", "dt_ln", "dt_ready", "dta_ready")
        cs_ready, end_ready, ex_ready = sems("cs_ready", "end_ready", "ex_ready")
        xdt_ready, xde_ready, st_upd = sems("xdt_ready", "xde_ready", "st_upd")
        arg_ready, exp_ready, wm_ready, y_ready, yn_ready = sems("arg_ready", "exp_ready", "wm_ready", "y_ready", "yn_ready")
        qa_ready, ckv_ready, kq_ready, kpe_ready = sems("qa_ready", "ckv_ready", "kq_ready", "kpe_ready")
        mx_ready, pr_exp, pr_ready = sems("mx_ready", "pr_exp", "pr_ready")
        ex8_arg, ex8_ready, sel_ready, route_ready = sems("ex8_arg", "ex8_ready", "sel_ready", "route_ready")
        moe_zero, ps_ready, pg_ready = sems("moe_zero", "ps_ready", "pg_ready")

        def kmaj(w):
            return w.rearrange("(k p) n -> p k n", p=P)

        chunks, where, released = [], {}, {}
        full_at = [0] * RING

        def chunk(label, *parts):
            s = len(chunks) % RING
            full_at[s] += 16 * len(parts)
            where[label] = (s, full_at[s])
            chunks.append((label, parts))

        def mod_chunks(layer):
            for j in range(12):
                chunk(("mod", layer, j), (0, kmaj(w_mod[layer])[:, :, 512 * j:512 * j + 512]))

        def ff_chunks(label, wg, wu, wd):
            for j, (f0, n) in enumerate(GU):
                chunk((label, "gu", j), (0, kmaj(wg)[:, :, P * f0:P * (f0 + n)]),
                      (2048, kmaj(wu)[:, :, P * f0:P * (f0 + n)]))
            for dp, fh in DN:
                chunk((label, "dn", dp, fh), (0, kmaj(wd)[:, FH * fh:FH * (fh + 1), 256 * dp:256 * dp + 256]))

        win = kmaj(w_in[0])
        mod_chunks(0)
        for j in range(4):
            chunk(("xbc", j), (0, win[:, :, D + 512 * j:D + 512 * j + 512]))
        V0 = D + 2048 + 32 + D
        for name, c0 in (("v", V0), ("u", V0 - D), ("z", 0)):
            for j in range(2):
                chunk((name, j), (0, win[:, :, c0 + 512 * j:c0 + 512 * j + 512]))
        for j in range(4):
            chunk(("wout", j), (0, kmaj(w_out[0])[:, :, 256 * j:256 * j + 256]))
        ff_chunks("ffn", ffn_w_gate[0], ffn_w_up[0], ffn_w_down[0])
        mod_chunks(1)
        chunk("dq", (0, kmaj(w_dq[0])))
        chunk("dkv", (0, kmaj(w_dkv[0])))
        chunk("ukv", (0, kmaj(w_ukv[0])))
        for j in range(2):
            chunk(("uq", j), (0, kmaj(w_uq[0])[:, :, 768 * j:768 * j + 768]))
        WO_PARTS = 2 + (-(len(chunks) + 2)) % RING
        WO_W = -(-D // (16 * WO_PARTS)) * 16
        WO_COLS = [(n, min(WO_W, D - n)) for n in range(0, D, WO_W)][:WO_PARTS]
        for j, (n0, w_) in enumerate(WO_COLS):
            chunk(("wo", j), (0, kmaj(w_o[0])[:, :, n0:n0 + w_]))
        assert len(chunks) % RING == 0 and sum(w_ for _, w_ in WO_COLS) == D
        STATIC = len(chunks)
        moe_base = list(full_at)
        ff_chunks("moe", moe_w_gate[0, 0], moe_w_up[0, 0], moe_w_down[0, 0])
        FULL_PER = [full_at[s] - moe_base[s] for s in range(RING)]
        MOE_CHUNKS = [l for l, _ in chunks[STATIC:]]
        del chunks[STATIC:]

        def part(label, k, n, at=0):
            return ring[:, where[label][0], at:at + k * n].rearrange("p (k n) -> p k n", k=k)

        fills, place, turn = [0] * BANKS, {}, [0]

        def filled(label):
            b, n = place[label]
            return bank_full[b], n

        def drained(label):
            b, n = place[label]
            return bank_free[b], n

        MOE_FILLS = ([("T", i) for i in range(6)] + [(s, f) for f in range(FT) for s in ("g", "u")]
                     + [("sc", i) for i in range(6)] + [("pgT", i) for i in range(NT)]
                     + [("ga", k) for k in range(KT)] + [("dn", k) for k in range(KT)])
        MOE_PER = [len(MOE_FILLS[b::BANKS]) for b in range(BANKS)]

        def moe_filled(label, e):
            b, n = place[("moe",) + label]
            return bank_full[b], e * MOE_PER[b] + n

        def moe_drained(label, e):
            b, n = place[("moe",) + label]
            return bank_free[b], e * MOE_PER[b] + n

        TILES = [("k", 3), ("k", 0), ("k", 1), ("k", 2), ("q", 0), ("q", 1), ("q", 2)]
        HEAD_TILES = [(h, t) for h in range(MH) for t in range(NT)]
        TURNS = [(t, g) for t in range(NT) for g in range(GROUPS)]
        w_release, sq_at, used_before_moe, added = {}, {}, [], {}
        ROOTS = ([("n", 0), "v", ("y", 0), ("y", 1), ("y", 2), ("n", 1), ("n", 2), "qa", "ckv"]
                 + [("kq", i) for i in range(7)] + [("n", 3)])

        def root_at(label):
            n = ROOTS.index(label)
            return n + 1, stat[:, 8 * n:8 * n + 8]

        const_dram = nc.inline_tensor(consts_np, name="tables").ap()
        iota_dram = nc.inline_tensor(np.tile(np.arange(TOK, dtype=np.float32), (P, 1)), name="slot_numbers").ap()
        block = ctx.enter_context(nc.Block())

        @block.tensor
        def _(pe):
            mm, tp = nc.tensor.matmul, nc.tensor.transpose

            def fill(label):
                b = turn[0] % BANKS
                turn[0] += 1
                fills[b] += 1
                place[label] = (b, fills[b])
                if fills[b] > 1:
                    pe.wait_ge(bank_free[b], fills[b] - 1)
                return PSUM[b], bank_full[b]

            def landed(label):
                pe.wait_ge(ring_full[where[label][0]], where[label][1])

            used = [0]

            def used_amid(label, last):
                used[0] += 1
                last.then_inc(chunk_used, 1)
                released[label] = (chunk_used, used[0])

            def blocks(label, sources):
                bank, full = fill(label)
                for k, src in enumerate(sources):
                    last = tp(bank[:, k * P:(k + 1) * P], src, ident)
                last.then_inc(full, 1)

            pe.wait_ge(const_loaded, 16)
            pe.wait_ge(prow_loaded, 16 * 8)
            bank, full = fill("col")
            tp(bank[:, 0:112], praw[0:112, 0, :], ident[0:112, 0:112])
            tp(bank[:, 112:223], praw[0:111, 1, :], ident[0:111, 0:111]).then_inc(full, 1)
            pe.wait_ge(wsp_loaded, 16)
            blocks("wsp", [praw[:, 2 + g, :] for g in range(SGRP)])

            def to_feature_major(n):
                for t in range(NT):
                    pe.wait_ge(xn_ready, NT * n + t + 1)
                    for half in range(2):
                        blocks(("nt", n, t, half), [XN[:, t, (4 * half + k) * P:(4 * half + k + 1) * P] for k in range(4)])

            def ht_ready(n):
                for t in range(NT):
                    pe.wait_ge(*drained(("nt", n, t, 0)))
                    pe.wait_ge(*drained(("nt", n, t, 1)))

            def modulation(layer):
                bank, full = fill(("mod", layer))
                for j in range(12):
                    label = ("mod", layer, j)
                    landed(label)
                    w = part(label, KT, 512)
                    for m in range(4):
                        o = bank[:, 2 * (4 * j + m):2 * (4 * j + m) + 2]
                        for k in range(KT):
                            last = mm(o, w[:, k, m * P:(m + 1) * P], sv[:, :, k], start=(k == 0), stop=(k == KT - 1))
                    if j < 11:
                        used_amid(label, last)
                last.then_inc(full, 1)
                released[("mod", layer, 11)] = filled(("mod", layer))

            def gate_rows(layer, which, n):
                pe.wait_ge(mod_ready, layer + 1)
                for s in range(2):
                    for half in range(2):
                        bank, full = fill(("gb", n, s, half))
                        for k in range(4):
                            m = which * KT + 4 * half + k
                            last = mm(bank[:, k * P:(k + 1) * P], modT[:, layer, m, s:s + 1].to_broadcast([P, P]), ident, start=True, stop=True)
                        last.then_inc(full, 1)

            def token_major(name, label, lhs, kt, width):
                landed(label)
                w = part(label, kt, width)
                for t in range(NT):
                    bank, full = fill((name, t))
                    for k in range(kt):
                        last = mm(bank[:, 0:width], lhs[:, k, t * P:(t + 1) * P], w[:, k, :], start=(k == 0), stop=(k == kt - 1))
                    last.then_inc(full, 1)
                released[label] = filled((name, NT - 1))

            to_feature_major(0)
            pe.wait_ge(sv_ready, 1)
            modulation(0)
            ht_ready(0)

            for j in range(4):
                label = ("xbc", j)
                landed(label)
                w = part(label, KT, 512)
                for m in range(4):
                    bank, full = fill(("xbc", 4 * j + m, "p"))
                    for k in range(KT):
                        last = mm(bank[:, 0:TOK], w[:, k, m * P:(m + 1) * P], HT[:, k, :], start=(k == 0), stop=(k == KT - 1))
                    last.then_inc(full, 1)
                released[label] = filled(("xbc", 4 * j + 3, "p"))
            pe.wait_ge(small_loaded, 16 * 9)
            bank, full = fill("dt")
            for t in range(NT):
                for k in range(KT):
                    last = mm(bank[:, 32 * t:32 * t + 32], HT[:, k, t * P:(t + 1) * P], wdt[:, k, :], start=(k == 0), stop=(k == KT - 1))
            last.then_inc(full, 1)
            for name in ("v", "u"):
                for j in range(2):
                    token_major((name, j, "p"), (name, j), HT, KT, 512)

            pe.wait_ge(*drained("wsp"))
            for t in range(NT):
                pe.wait_ge(vn_ready, t + 1)
                for half in range(2):
                    bank, full = fill(("sg", t, half))
                    for g in range(2):
                        gg = 2 * half + g
                        last = mm(bank[:, g * SGD:(g + 1) * SGD], wspT[:, gg, :], V[:, t, gg * SGD:(gg + 1) * SGD], start=True, stop=True)
                    last.then_inc(full, 1)
            for j in range(2):
                token_major(("z", j, "p"), ("z", j), HT, KT, 512)

            pe.wait_ge(cv_ready, 12)
            for t in range(NT):
                for q in range(3):
                    blocks(("xs", t, q), [CV[:, 4 * q + k, TOK0[t]:TOK0[t] + P] for k in range(4)])
            pe.wait_ge(dta_ready, 1)
            bank, full = fill("cs")
            for t in range(NT):
                for d in range(2):
                    o = 32 * t + 16 * d
                    mm(bank[:, o:o + 16], tri[d], dtA[:, o:o + 16], start=True, stop=True)
            mm(bank[:, 96:192], ones, dtA, start=True, stop=True).then_inc(full, 1)
            pe.wait_ge(cv_ready, CCT)
            for t in range(NT):
                bank, full = fill(("cb", t))
                for g in range(GROUPS):
                    last = mm(bank[:, g * P:(g + 1) * P], CV[:, 8 + g, TOK0[t]:TOK0[t] + P], CV[:, 12 + g, TOK0[t]:TOK0[t] + P], start=True, stop=True)
                last.then_inc(full, 1)
            pe.wait_ge(st_loaded, 16)
            for d in range(2):
                for half in range(2):
                    blocks(("st", d, half), [st_raw[:, d, 4 * half + k, :] for k in range(4)])
            for t in range(NT):
                pe.wait_ge(*drained(("xs", t, 2)))
            for d in range(2):
                pe.wait_ge(xde_ready, d + 1)
                for half in range(2):
                    bank, full = fill(("cst", d, half))
                    for k in range(4):
                        i = 4 * half + k
                        last = mm(bank[:, k * P:(k + 1) * P], W[:, d, i * P:(i + 1) * P], BT[:, 0, (i // 2) * P:(i // 2 + 1) * P], start=True, stop=True)
                    last.then_inc(full, 1)

            def state_output(t, d):
                for half in range(2):
                    bank, full = fill(("off", t, d, half))
                    for g in range(2):
                        gg = 2 * half + g
                        last = mm(bank[:, g * 256:(g + 1) * 256], CV[:, 12 + gg, TOK0[t]:TOK0[t] + P], stT[:, d, gg * 256:(gg + 1) * 256], start=True, stop=True)
                    last.then_inc(full, 1)

            for d in range(2):
                pe.wait_ge(*drained(("st", d, 0)))
                pe.wait_ge(*drained(("st", d, 1)))
            state_output(1, 0)
            state_output(2, 1)
            for d in range(2):
                pe.wait_ge(xde_ready, 3 + d)
                for half in range(2):
                    bank, full = fill(("own", d, half))
                    for g in range(2):
                        gg = 2 * half + g
                        last = mm(bank[:, g * 256:(g + 1) * 256], BT[:, 1 + d, gg * P:(gg + 1) * P], W[:, d, gg * 256:(gg + 1) * 256], start=True, stop=True)
                    last.then_inc(full, 1)
            for d in range(2):
                pe.wait_ge(st_upd, d + 1)
                state_output(2 - d, d)

            def decay_rows(i):
                t, g = TURNS[i]
                for d in range(2):
                    bank, full = fill(("cr", i, d))
                    for h in range(HPG):
                        col = 32 * t + 16 * d + HPG * g + h
                        last = mm(bank[:, h * P:(h + 1) * P], dtA[:, col:col + 1].to_broadcast([P, P]), tri[d], start=True, stop=True)
                    last.then_inc(full, 1)

            pe.wait_ge(xdt_ready, 6)
            decay_rows(0)
            for i, (t, g) in enumerate(TURNS):
                if i + 1 < len(TURNS):
                    decay_rows(i + 1)
                if g % 2 == 0:
                    bank, full = fill(("y", t, g // 2))
                pe.wait_ge(wm_ready, i + 1)
                for h in range(HPG):
                    hh = HPG * g + h
                    for d in range(2):
                        last = mm(bank[:, (hh % 8) * HD:(hh % 8 + 1) * HD], W[:, i % 2, (4 * d + h) * P:(4 * d + h + 1) * P],
                                  xdt[:, t, d, hh * HD:(hh + 1) * HD], start=(d == 0), stop=(d == 1))
                if g % 2 == 0:
                    last.then_inc(w_used, 1)
                    w_release[i] = (w_used, i // 2 + 1)
                else:
                    last.then_inc(full, 1)
                    w_release[i] = filled(("y", t, g // 2))

            gate_rows(0, 2, 0)
            for t in range(NT):
                for half in range(2):
                    blocks(("yu", t, half), [U[:, t, (4 * half + k) * P:(4 * half + k + 1) * P] for k in range(4)])
            for t in range(NT):
                pe.wait_ge(yn_ready, t + 1)
                for half in range(2):
                    blocks(("yy", t, half), [XS[:, t, (4 * half + k) * P:(4 * half + k + 1) * P] for k in range(4)])
            for t in range(NT):
                for half in range(2):
                    pe.wait_ge(*drained(("yu", t, half)))
                    pe.wait_ge(*drained(("yy", t, half)))
            for j in range(4):
                token_major(("wout", j, "p"), ("wout", j), YT, 16, 256)

            to_feature_major(1)
            gate_rows(0, 5, 1)
            ht_ready(1)
            for j, (f0, n) in enumerate(GU):
                label = ("ffn", "gu", j)
                landed(label)
                for m in range(n):
                    for name, at in (("g", 0), ("u", 2048)):
                        w = part(label, KT, n * P, at)
                        bank, full = fill((name, f0 + m))
                        for k in range(KT):
                            last = mm(bank[:, 0:TOK], w[:, k, m * P:(m + 1) * P], HT[:, k, :], start=(k == 0), stop=(k == KT - 1))
                        last.then_inc(full, 1)
                released[label] = filled(("u", f0 + n - 1))
            pe.wait_ge(*drained(("u", FT - 1)))
            pe.wait_ge(*drained(("u", FT - 2)))
            for dp in range(4):
                banks = [fill(("down", dp, t)) for t in range(NT)]
                for fh in range(2):
                    label = ("ffn", "dn", dp, fh)
                    landed(label)
                    w = part(label, FH, 256)
                    for t in range(NT):
                        for f in range(FH):
                            last = mm(banks[t][0][:, 0:256], aT[:, FH * fh + f, t * P:(t + 1) * P], w[:, f, :],
                                      start=(fh == 0 and f == 0), stop=(fh == 1 and f == FH - 1))
                        if fh == 1:
                            last.then_inc(banks[t][1], 1)
                    if fh == 0:
                        used_amid(label, last)
                    else:
                        released[label] = filled(("down", dp, NT - 1))

            modulation(1)
            to_feature_major(2)
            gate_rows(1, 2, 2)
            ht_ready(2)
            token_major("dq_p", "dq", HT, KT, QR)
            token_major("dkv_p", "dkv", HT, KT, KVR + ROPE)
            for t in (3, 0, 1, 2):
                if t == 3:
                    pe.wait_ge(cache_loaded, 32)
                else:
                    pe.wait_ge(ckv_ready, t + 1)
                blocks(("ckvT", t), [ckv[:, t, k * P:(k + 1) * P] for k in range(2)])
            for t in range(NT):
                pe.wait_ge(qa_ready, t + 1)
                blocks(("qaT", t), [qa[:, t, k * P:(k + 1) * P] for k in range(3)])

            def expand(i):
                kind, t = TILES[i]
                if kind == "k":
                    if i == 0:
                        landed("ukv")
                    pe.wait_ge(*drained(("ckvT", t)))
                    w = part("ukv", 2, 2048)
                    for j in range(4):
                        bank, full = fill(("kv", t, j))
                        for k in range(2):
                            last = mm(bank[:, :], ckvT[:, k, t * P:(t + 1) * P], w[:, k, 512 * j:512 * j + 512], start=(k == 0), stop=(k == 1))
                        last.then_inc(full, 1)
                    released["ukv"] = filled(("kv", t, 3))
                else:
                    pe.wait_ge(*drained(("qaT", t)))
                    for j in range(4):
                        if t == 0 and j % 2 == 0:
                            landed(("uq", j // 2))
                        w = part(("uq", j // 2), 3, 768)
                        bank, full = fill(("q", t, j))
                        for k in range(3):
                            last = mm(bank[:, 0:384], qaT[:, k, t * P:(t + 1) * P], w[:, k, 384 * (j % 2):384 * (j % 2) + 384], start=(k == 0), stop=(k == 2))
                        last.then_inc(full, 1)
                        released[("uq", j // 2)] = filled(("q", t, j))

            expand(0)
            for i in range(len(TILES)):
                if i + 1 < len(TILES):
                    expand(i + 1)
                pe.wait_ge(kq_ready, i + 1)
                for q in range(2):
                    blocks(("hT", i, q), [KQN[:, i % 2, 4 * q + k, :] for k in range(4)])
                blocks(("hT", i, 2), [kq_v[:, i % 2, D + k * P:D + (k + 1) * P] for k in range(4)])

            for i in range(len(TILES)):
                for q in range(3):
                    pe.wait_ge(*drained(("hT", i, q)))

            def scores(n):
                h, t = HEAD_TILES[n]
                bank, full = fill(("s", n))
                r = 64 * (h % 2)
                k0, kn = (0, P) if t == 0 else (P, 3 * P)
                mm(bank[:, 0:kn], qTn[:, h, t * P:(t + 1) * P], kTn[:, h, k0:k0 + kn], start=True, stop=False)
                mm(bank[:, 0:kn], qTr[r:r + 64, h // 2, t * P:(t + 1) * P], kTr[r:r + 64, h // 2, k0:k0 + kn],
                   start=False, stop=True).then_inc(full, 1)

            def values(h):
                for t in range(NT):
                    pe.wait_ge(*drained(("pT", NT * h + t)))
                bank, full = fill(("o", h))
                mm(bank[:, 0:P], VV[:, 0, h * VH:(h + 1) * VH], PT[:, h % 2, 0:P], start=True, stop=True)
                for k in range(3):
                    last = mm(bank[:, P:3 * P], VV[:, 1 + k, h * VH:(h + 1) * VH], PT[:, h % 2, P + 256 * k:P + 256 * k + 256],
                              start=(k == 0), stop=(k == 2))
                last.then_inc(full, 1)

            scores(0)
            for n, (h, t) in enumerate(HEAD_TILES):
                if n + 1 < len(HEAD_TILES):
                    scores(n + 1)
                pe.wait_ge(pr_ready, n + 1)
                blocks(("pT", n), [PR[:, n % 2, k * P:(k + 1) * P] for k in range(1 if t == 0 else 3)])
                if t == 0 and h > 0:
                    values(h - 1)
            values(MH - 1)
            for h in range(MH):
                pe.wait_ge(*drained(("o", h)))
            for j, (_, w_) in enumerate(WO_COLS):
                token_major(("wo", j, "p"), ("wo", j), OT, KT, w_)

            to_feature_major(3)
            ht_ready(3)
            bank, full = fill("lg")
            for t in range(NT):
                for k in range(KT):
                    last = mm(bank[:, 8 * t:8 * t + 8], HT[:, k, t * P:(t + 1) * P], wrt[:, k, :], start=(k == 0), stop=(k == KT - 1))
            last.then_inc(full, 1)
            for t in range(NT):
                for half in range(2):
                    blocks(("h2", t, half), [HT[:, 4 * half + k, t * P:(t + 1) * P] for k in range(4)])
            pe.wait_ge(sel_ready, 1)
            bank, full = fill("rank")
            for t in range(NT):
                for s in range(t + 1):
                    mm(bank[:, 8 * t:8 * t + 8], before if s == t else ones, sel[:, s, :], start=(s == 0), stop=(s == t))
            for s in range(NT):
                last = mm(bank[:, 24:32], ones, sel[:, s, :], start=(s == 0), stop=(s == NT - 1))
            last.then_inc(full, 1)
            for t in range(NT):
                pe.wait_ge(*drained(("h2", t, 0)))
                pe.wait_ge(*drained(("h2", t, 1)))
            pe.wait_ge(ps_ready, 1)
            for k in range(KT):
                bank, full = fill(("ga0", k))
                for t in range(NT):
                    last = mm(bank[:, 0:TOK], H2[:, t, k * P:(k + 1) * P], PS[:, t, :], start=(t == 0), stop=(t == NT - 1))
                last.then_inc(full, 1)

            for i, label in enumerate(MOE_FILLS):
                place[("moe",) + label] = (i % BANKS, fills[i % BANKS] + i // BANKS + 1)

            def moe_bank(label, e):
                b, n = place[("moe",) + label]
                pe.wait_ge(bank_free[b], e * MOE_PER[b] + (n - 1))
                return PSUM[b], bank_full[b]

            def moe_landed(label, e):
                s, n = where[label]
                pe.wait_ge(ring_full[s], e * FULL_PER[s] + n)

            def turn_outputs(e):
                for i in range(6):
                    bank, full = moe_bank(("T", i), e)
                    for k in range(4):
                        last = tp(bank[:, k * P:(k + 1) * P], yT[:, 4 * (i % 2) + k, (i // 2) * P:(i // 2 + 1) * P], ident)
                    last.then_inc(full, 1)

            def scatter(e, slot_tiles):
                for i in range(6):
                    t, half = i // 2, i % 2
                    bank, full = moe_bank(("sc", i), e)
                    for s in range(slot_tiles):
                        last = mm(bank[:, :], PGT[:, s, t * P:(t + 1) * P], yt[:, s, 512 * half:512 * half + 512],
                                  start=(s == 0), stop=(s == slot_tiles - 1))
                    last.then_inc(full, 1)

            def hidden(e, N):
                for j, (f0, n) in enumerate(GU):
                    label = ("moe", "gu", j)
                    moe_landed(label, e)
                    for m in range(n):
                        for name, at in (("g", 0), ("u", 2048)):
                            w = part(label, KT, n * P, at)
                            bank, full = moe_bank((name, f0 + m), e)
                            for k in range(KT):
                                last = mm(bank[:, 0:N], w[:, k, m * P:(m + 1) * P], xeT[:, k, 0:N], start=(k == 0), stop=(k == KT - 1))
                            last.then_inc(full, 1)

            def gather(e, N):
                for k in range(KT):
                    bank, full = moe_bank(("ga", k), e)
                    for t in range(NT):
                        last = mm(bank[:, 0:N], H2[:, t, k * P:(k + 1) * P], PS[:, t, 0:N], start=(t == 0), stop=(t == NT - 1))
                    last.then_inc(full, 1)

            def output(e, N):
                for dp in range(4):
                    banks = [moe_bank(("dn", 2 * dp + m), e) for m in range(2)]
                    for fh in range(2):
                        label = ("moe", "dn", dp, fh)
                        moe_landed(label, e)
                        w = part(label, FH, 256)
                        for m in range(2):
                            for f in range(FH):
                                last = mm(banks[m][0][:, 0:N], w[:, f, m * P:(m + 1) * P], aT[:, FH * fh + f, 0:N],
                                          start=(fh == 0 and f == 0), stop=(fh == 1 and f == FH - 1))
                            if fh == 1:
                                last.then_inc(banks[m][1], 1)
                        if fh == 0:
                            last.then_inc(chunk_used, 1)

            used_before_moe.append(used[0])
            pe.wait_ge(route_ready, 1)
            pe.wait_ge(moe_zero, 3)
            with pe.Fori(0, NE) as e:
                this = pe.value_load(vtab[0:1, 0, bass.ds(e + 1, 1)], min_val=0, max_val=len(WIDTHS) - 1)
                nxt = pe.value_load(vtab[0:1, 0, bass.ds(e + 2, 1)], min_val=0, max_val=len(WIDTHS) - 1)
                prev_tiles = pe.value_load(vtab[0:1, 1, bass.ds(e, 1)], min_val=1, max_val=NT)
                for k in range(KT):
                    pe.wait_ge(*moe_drained(("dn", k), e - 1))
                turn_outputs(e)
                for k in range(KT):
                    pe.wait_ge(*moe_drained(("ga", k), e - 1))
                for v, N in enumerate(WIDTHS):
                    with pe.If(this == v):
                        hidden(e, N)
                for i in range(6):
                    pe.wait_ge(*moe_drained(("T", i), e))
                for i in range(NT):
                    pe.wait_ge(*moe_drained(("pgT", i), e - 1))
                for n in range(1, NT + 1):
                    with pe.If(prev_tiles == n):
                        scatter(e, n)
                pe.wait_ge(pg_ready, e + 1)
                for i in range(NT):
                    bank, full = moe_bank(("pgT", i), e)
                    for t in range(NT):
                        last = tp(bank[:, t * P:(t + 1) * P], PG[:, t, i * P:(i + 1) * P], ident)
                    last.then_inc(full, 1)
                pe.wait_ge(ps_ready, e + 2)
                for v, N in enumerate(WIDTHS):
                    with pe.If(nxt == v):
                        gather(e, N)
                pe.wait_ge(*moe_drained(("u", FT - 2), e))
                pe.wait_ge(*moe_drained(("u", FT - 1), e))
                for v, N in enumerate(WIDTHS):
                    with pe.If(this == v):
                        output(e, N)
            for b in range(BANKS):
                fills[b] += NE * MOE_PER[b]
            for k in range(KT):
                pe.wait_ge(*moe_drained(("dn", k), NE - 1))
            for i in range(6):
                blocks(("lastT", i), [yT[:, 4 * (i % 2) + k, (i // 2) * P:(i // 2 + 1) * P] for k in range(4)])
            gate_rows(1, 5, 3)
            for i in range(6):
                pe.wait_ge(*drained(("lastT", i)))
            for i in range(NT):
                pe.wait_ge(*moe_drained(("pgT", i), NE - 1))
            for i in range(6):
                t, half = i // 2, i % 2
                bank, full = fill(("last", i))
                for s in range(NT):
                    last = mm(bank[:, :], PGT[:, s, t * P:(t + 1) * P], yt[:, s, 512 * half:512 * half + 512], start=(s == 0), stop=(s == NT - 1))
                last.then_inc(full, 1)

        @block.scalar
        def _(act):
            act_fn = nc.scalar.activation
            squares = [0]

            def copy(out, in_):
                return act_fn(out, in_, ACT.Copy)

            def square_sum(label, col, src, junk_):
                if label[0] != "n":
                    act.wait_ge(sq_done, squares[0])
                squares[0] += 1
                sq_at[label] = squares[0]
                act_fn(junk_, src, ACT.Square, accum_out=root_at(label)[1][:, col:col + 1]).then_inc(sq_done, 1)

            def root(label, n):
                i, cols = root_at(label)
                act.wait_ge(ms_ready, i)
                act_fn(cols[:, 0:n], cols[:, 0:n], ACT.Sqrt).then_inc(rt_ready, 1)

            def evacuate(label, pairs):
                act.wait_ge(*filled(label))
                for out, src in pairs:
                    last = copy(out, src)
                last.then_inc(drained(label)[0], 1)

            def bank_of(label):
                return PSUM[place[label][0]]

            def norm_squares(n):
                for t in range(NT):
                    square_sum(("n", n), t, X[:, t, :], XN[:, t, :])

            def modulated(n, layer, i):
                for t in range(NT):
                    s = 0 if t == 0 else 1
                    label = ("nt", n, t, 0)
                    act.wait_ge(*filled(label))
                    for k in range(4):
                        last = act_fn(HT[:, k, t * P:(t + 1) * P], bank_of(label)[:, k * P:(k + 1) * P], ACT.Identity,
                                      bias=modT[:, layer, i * KT + k, s:s + 1], scale=modT[:, layer, (i + 1) * KT + k, s:s + 1])
                    last.then_inc(drained(label)[0], 1)

            def gates(n):
                for s in range(2):
                    for half in range(2):
                        evacuate(("gb", n, s, half), [(GB[:, s, 512 * half:512 * half + 512], bank_of(("gb", n, s, half))[:, :])])

            act.dma_start(CST[:, :], const_dram).then_inc(const_loaded, 16)
            act.dma_start(praw[0:8, 0, :], c_ctx.rearrange("(k p) -> k p", p=P)).then_inc(prow_loaded, 16)
            act.dma_start(praw[8:16, 0, :], c[0].rearrange("(k p) -> k p", p=P)).then_inc(prow_loaded, 16)
            act.dma_start(praw[16:112, 0, :], b_mod.rearrange("l (m p) -> (l m) p", p=P)).then_inc(prow_loaded, 16)
            act.dma_start(praw[0:80, 1, :], conv_w[0].rearrange("i (c p) -> (i c) p", p=P)).then_inc(prow_loaded, 16)
            act.dma_start(praw[80:96, 1, :], conv_b[0].rearrange("(c p) -> c p", p=P)).then_inc(prow_loaded, 16)
            act.dma_start(praw[96:104, 1, :], ssd_norm[0].rearrange("(c p) -> c p", p=P)).then_inc(prow_loaded, 16)
            act.dma_start(praw[104:108, 1, :], b_sp[0]).then_inc(prow_loaded, 16)
            act.dma_start(praw[108:111, 1, :], q_a_norm[0].rearrange("(c p) -> c p", p=P)).then_inc(prow_loaded, 16)
            act.dma_start(praw[:, 2:6, :], w_sp[0].rearrange("g t s -> t g s")).then_inc(wsp_loaded, 16)

            for out, src in ((dtb_r, dt_bias.rearrange("a d h -> a (d h)")), (alog_r, a_log.rearrange("a d h -> a (d h)")),
                             (dsk_r, d_skip), (qn_r, q_norm), (kn_r, k_norm), (kvn_r, kv_a_norm), (sgn_r, sgu_norm)):
                act.dma_start(out, src.to_broadcast([P, src.shape[1]])).then_inc(small_loaded, 16)
            act.dma_start(wdt[:, :, :], win[:, :, 3072:3104]).then_inc(small_loaded, 16)
            act.dma_start(wrt[:, :, :], kmaj(router[0])).then_inc(small_loaded, 16)

            act.wait_ge(x_loaded, 32)
            norm_squares(0)
            root(("n", 0), NT)
            act.wait_ge(*drained("col"))
            act_fn(sv[:, :, :].rearrange("p s k -> p (s k)"), colT[:, 0, 0:16], ACT.Silu).then_inc(sv_ready, 1)
            evacuate("wsp", [(wspT[:, :, :].rearrange("p g t -> p (g t)"), bank_of("wsp")[:, :])])
            act.wait_ge(mod_ready, 1)
            modulated(0, 0, 0)

            def conv_silu(ct):
                act.wait_ge(conv_done, ct + 1)
                act_fn(CV[:, ct, :], CV[:, ct, :], ACT.Silu).then_inc(cv_ready, 1)

            act.wait_ge(raw_zero, 1)
            for ct in range(CCT):
                if ct >= 4:
                    act.wait_ge(conv_done, ct - 3)
                b = bank_of(("xbc", ct, "p"))
                evacuate(("xbc", ct, "p"), [(raw[:, ct % 4, PAD:PAD + P], b[:, 0:P]),
                                            (raw[:, ct % 4, 2 * PAD + P:2 * PAD + P + LAT], b[:, P:TOK])])
                if ct >= 2:
                    conv_silu(ct - 2)
            conv_silu(14)
            conv_silu(15)
            act.wait_ge(dt_arg, 1)
            act_fn(dtu, dtw, ACT.Exp).then_inc(dt_exp, 1)
            act.wait_ge(small_loaded, 16 * 9)
            act_fn(aexp, alog_r, ACT.Exp).then_inc(dt_exp, 1)
            act.wait_ge(dt_w, 1)
            act_fn(dtv, dtw, ACT.Ln).then_inc(dt_ln, 1)
            for j in range(2):
                for t in range(NT):
                    evacuate((("v", j, "p"), t), [(V[:, t, 512 * j:512 * j + 512], bank_of((("v", j, "p"), t))[:, :])])
            for t in range(NT):
                for j in range(2):
                    act.wait_ge(*drained((("v", j, "p"), t)))
                square_sum("v", t, V[:, t, :], Z[:, t, :])
            root("v", NT)
            for j in range(2):
                for t in range(NT):
                    evacuate((("u", j, "p"), t), [(U[:, t, 512 * j:512 * j + 512], bank_of((("u", j, "p"), t))[:, :])])
            for j in range(2):
                for t in range(NT):
                    label = (("z", j, "p"), t)
                    act.wait_ge(*filled(label))
                    act_fn(Z[:, t, 512 * j:512 * j + 512], bank_of(label)[:, :], ACT.Silu).then_inc(drained(label)[0], 1)
            for t in range(NT):
                evacuate(("xs", t, 0), [(XS[:, t, 0:512], bank_of(("xs", t, 0))[:, :])])
                evacuate(("xs", t, 2), [(BT[:, t, :], bank_of(("xs", t, 2))[:, :])])
            act.wait_ge(cs_ready, 1)
            act_fn(ecs, csn, ACT.Exp, scale=-1.0).then_inc(ex_ready, 1)
            act.wait_ge(end_ready, 1)
            act_fn(den, den, ACT.Exp).then_inc(ex_ready, 1)
            act_fn(etot, tot, ACT.Exp).then_inc(ex_ready, 1)
            for t in range(NT):
                evacuate(("cb", t), [(cb[:, t, :, :].rearrange("p g l -> p (g l)"), bank_of(("cb", t))[:, :])])
            for d in range(2):
                for half in range(2):
                    evacuate(("st", d, half), [(stT[:, d, 512 * half:512 * half + 512], bank_of(("st", d, half))[:, :])])
            for d in range(2):
                for half in range(2):
                    evacuate(("cst", d, half), [(cst[:, d, 4 * half:4 * half + 4, :].rearrange("p i n -> p (i n)"), bank_of(("cst", d, half))[:, :])])
            for i in range(len(TURNS)):
                act.wait_ge(arg_ready, i + 1)
                act_fn(W[:, i % 2, :], W[:, i % 2, :], ACT.Exp).then_inc(exp_ready, 1)
            gates(0)
            act.wait_ge(state_out, 32)
            for t in range(NT):
                for half in range(2):
                    label = ("yu", t, half)
                    evacuate(label, [(YT[:, 8 + 4 * half:12 + 4 * half, t * P:(t + 1) * P], bank_of(label)[:, :].rearrange("p (k t) -> p k t", k=4))])
            for t in range(NT):
                act.wait_ge(y_ready, t + 1)
                square_sum(("y", t), 0, XS[:, t, :], sgn_r)
                root(("y", t), 1)
            for t in range(NT):
                label = ("yy", t, 0)
                act.wait_ge(*filled(label))
                for k in range(4):
                    last = act_fn(YT[:, k, t * P:(t + 1) * P], bank_of(label)[:, k * P:(k + 1) * P], ACT.Copy, scale=ssdn[:, k:k + 1])
                last.then_inc(drained(label)[0], 1)

            act.wait_ge(x_updated, 1)
            norm_squares(1)
            root(("n", 1), NT)
            modulated(1, 0, 3)
            gates(1)
            for f in range(FT):
                act.wait_ge(*filled(("g", f)))
                if f >= 2:
                    act.wait_ge(*drained(("u", f - 2)))
                act_fn(sg[:, f % 2, :], bank_of(("g", f))[:, 0:TOK], ACT.Silu).then_inc(drained(("g", f))[0], 1)

            act.wait_ge(x_updated, 2)
            norm_squares(2)
            root(("n", 2), NT)
            act.wait_ge(mod_ready, 2)
            modulated(2, 1, 0)
            gates(2)
            for t in range(NT):
                evacuate(("dq_p", t), [(qa[:, t, :], bank_of(("dq_p", t))[:, 0:QR])])
            for t in range(NT):
                act.wait_ge(*drained(("dq_p", t)))
                square_sum("qa", t, qa[:, t, :], junk[:, 0:QR])
            root("qa", NT)
            for t in range(NT):
                evacuate(("dkv_p", t), [(ckv[:, t, :], bank_of(("dkv_p", t))[:, 0:KVR]), (kpe[:, t, :], bank_of(("dkv_p", t))[:, KVR:KVR + ROPE])])
            for t in range(NT):
                act.wait_ge(*drained(("dkv_p", t)))
                square_sum("ckv", t, ckv[:, t, :], junk[:, QR:QR + KVR])
            root("ckv", NT)
            for t in (3, 0, 1, 2):
                evacuate(("ckvT", t), [(ckvT[:, :, t * P:(t + 1) * P], bank_of(("ckvT", t))[:, 0:2 * P].rearrange("p (k t) -> p k t", k=2))])
            for t in range(NT):
                label = ("qaT", t)
                act.wait_ge(*filled(label))
                for k in range(3):
                    last = act_fn(qaT[:, k, t * P:(t + 1) * P], bank_of(label)[:, k * P:(k + 1) * P], ACT.Copy, scale=qanc[:, k:k + 1])
                last.then_inc(drained(label)[0], 1)

            def expanded(i):
                kind, t = TILES[i]
                if i >= 2:
                    act.wait_ge(*filled(("hT", i - 2, 2)))
                for j in range(4):
                    if kind == "k":
                        b = bank_of(("kv", t, j))[:, :].rearrange("p (h n) -> p h n", h=2)
                        evacuate(("kv", t, j), [(KQN[:, i % 2, 2 * j:2 * j + 2, :], b[:, :, 0:NOPE]),
                                                (VV[:, t, 256 * j:256 * j + 256].rearrange("p (h n) -> p h n", h=2), b[:, :, NOPE:])])
                    else:
                        b = bank_of(("q", t, j))[:, 0:384].rearrange("p (h n) -> p h n", h=2)
                        evacuate(("q", t, j), [(KQN[:, i % 2, 2 * j:2 * j + 2, :], b[:, :, 0:NOPE]),
                                               (KQR[:, i % 2, 2 * j:2 * j + 2, :], b[:, :, NOPE:])])
                if kind == "k":
                    act.wait_ge(ckv_ready, 3)
                    if t == 3:
                        act.wait_ge(cache_loaded, 32)
                    copy(KQR[:, i % 2, :, :], kpe[:, t, :].unsqueeze(1).broadcast_to([P, MH, ROPE])).then_inc(kpe_ready, 1)
                    act.wait_ge(kpe_ready, i + 1)
                for j in range(4):
                    act.wait_ge(*drained((kind if kind == "q" else "kv", t, j)))
                if i > 0:
                    act.wait_ge(kq_ready, i)
                squares[0] += 1
                sq_at[("kq", i)] = squares[0]
                act_fn(junk, kq_v[:, i % 2, :], ACT.Square).then_inc(sq_done, 1)
                root(("kq", i), MH)

            def turned(i):
                kind, t = TILES[i]
                n_to, r_to = (kTn, kTr) if kind == "k" else (qTn, qTr)
                evacuate(("hT", i, 0), [(n_to[:, 0:4, t * P:(t + 1) * P], bank_of(("hT", i, 0))[:, :].rearrange("p (k t) -> p k t", k=4))])
                evacuate(("hT", i, 2), [(r_to[:, :, t * P:(t + 1) * P], bank_of(("hT", i, 2))[:, :].rearrange("p (k t) -> p k t", k=4))])

            for i in range(len(TILES)):
                expanded(i)
                if i > 0:
                    turned(i - 1)
            turned(len(TILES) - 1)

            def probs_turned(n):
                h, t = HEAD_TILES[n]
                b = bank_of(("pT", n))
                if t == 0:
                    pair = (PT[:, h % 2, 0:P], b[:, 0:P])
                else:
                    pair = (PT[:, h % 2, P:896].rearrange("p (k q) -> p k q", k=3)[:, :, (t - 1) * P:t * P],
                            b[:, 0:TOK].rearrange("p (k q) -> p k q", k=3))
                evacuate(("pT", n), [pair])

            for n, (h, t) in enumerate(HEAD_TILES):
                kn = P if t == 0 else TOK
                act.wait_ge(mx_ready, n + 1)
                if n >= 2:
                    act.wait_ge(*filled(("pT", n - 2)))
                act_fn(PR[:, n % 2, 0:kn], bank_of(("s", n))[:, 0:kn], ACT.Exp, bias=nmx[:, n:n + 1], scale=QK ** -0.5,
                       accum_out=psum_[:, n:n + 1]).then_inc(drained(("s", n))[0], 1)
                if n > 0:
                    probs_turned(n - 1)
            probs_turned(len(HEAD_TILES) - 1)

            act.wait_ge(x_updated, 3)
            norm_squares(3)
            root(("n", 3), NT)
            modulated(3, 1, 3)
            act.wait_ge(ex8_arg, 1)
            act_fn(gpair[:, 0:3], gpair[:, 0:3], ACT.Exp).then_inc(ex8_ready, 1)
            for t in range(NT):
                evacuate(("h2", t, 0), [(H2[:, t, 0:512], bank_of(("h2", t, 0))[:, :])])
            for k in range(KT):
                evacuate(("ga0", k), [(xeT[:, k, :], bank_of(("ga0", k))[:, 0:TOK])])

            def moe_evacuate(label, e, out, in_):
                act.wait_ge(*moe_filled(label, e))
                copy(out, in_).then_inc(moe_drained(label, e)[0], 1)

            def moe_bank_of(label):
                return PSUM[place[("moe",) + label][0]]

            with act.Fori(0, NE) as e:
                for i in (0, 2, 4):
                    moe_evacuate(("T", i), e, yt[:, i // 2, 0:512], moe_bank_of(("T", i))[:, :])
                for f in range(FT):
                    act.wait_ge(*moe_filled(("g", f), e))
                    if f >= 2:
                        act.wait_ge(*moe_drained(("u", f - 2), e))
                    act_fn(sg[:, f % 2, :], moe_bank_of(("g", f))[:, 0:TOK], ACT.Silu).then_inc(moe_drained(("g", f), e)[0], 1)
                for i in range(NT):
                    moe_evacuate(("pgT", i), e, PGT[:, i, :], moe_bank_of(("pgT", i))[:, 0:TOK])
                for k in range(KT):
                    moe_evacuate(("ga", k), e, xeT[:, k, :], moe_bank_of(("ga", k))[:, 0:TOK])
                for k in (1, 3, 5, 7):
                    moe_evacuate(("dn", k), e, yT[:, k, :], moe_bank_of(("dn", k))[:, 0:TOK])
            for i in (0, 2, 4):
                evacuate(("lastT", i), [(yt[:, i // 2, 0:512], bank_of(("lastT", i))[:, :])])
            gates(3)

        @block.vector
        def _(dve):
            v = nc.vector
            steps = [0]

            def then(ins):
                steps[0] += 1
                ins.then_inc(dve_step, 1)
                dve.wait_ge(dve_step, steps[0])

            def note(ins):
                steps[0] += 1
                ins.then_inc(dve_step, 1)
                return steps[0]

            def bank_of(label):
                return PSUM[place[label][0]]

            def inverse_root(label, n, width):
                i, cols = root_at(label)
                cols = cols[:, 0:n]
                v.tensor_scalar(cols, cols, 1.0 / width, EPS, ALU.mult, ALU.add).then_inc(ms_ready, 1)
                dve.wait_ge(rt_ready, i)
                then(v.reciprocal(cols, cols))
                return root_at(label)[1]

            def normalise(n):
                dve.wait_ge(sq_done, sq_at[("n", n)])
                r = inverse_root(("n", n), NT, D)
                for t in range(NT):
                    v.tensor_scalar(XN[:, t, :], X[:, t, :], r[:, t:t + 1], None, ALU.mult).then_inc(xn_ready, 1)

            def modulated(n, layer, i):
                for t in range(NT):
                    s = 0 if t == 0 else 1
                    label = ("nt", n, t, 1)
                    dve.wait_ge(*filled(label))
                    for k in range(4, 8):
                        last = v.tensor_scalar(HT[:, k, t * P:(t + 1) * P], bank_of(label)[:, (k - 4) * P:(k - 3) * P],
                                               modT[:, layer, (i + 1) * KT + k, s:s + 1], modT[:, layer, i * KT + k, s:s + 1], ALU.mult, ALU.add)
                    last.then_inc(drained(label)[0], 1)

            def add_bias(layer):
                dve.wait_ge(*filled(("mod", layer)))
                ins = v.tensor_tensor(modT[:, layer, :, :], bank_of(("mod", layer))[:, 0:96].rearrange("p (m s) -> p m s", s=2),
                                      bmodc[:, layer, :].unsqueeze(2).broadcast_to([P, NMOD, 2]), ALU.add)
                ins.then_inc(drained(("mod", layer))[0], 1)
                dve.wait_ge(*drained(("mod", layer)))
                for i in (1, 4):
                    sc = modT[:, layer, i * KT:(i + 1) * KT, :]
                    last = v.tensor_scalar(sc, sc, 1.0, None, ALU.add)
                last.then_inc(mod_ready, 1)
                dve.wait_ge(mod_ready, layer + 1)

            def gated_update(name, j, n0, width, final, n):
                if j == 0:
                    added.clear()
                for t in range(NT):
                    s = 0 if t == 0 else 1
                    label = (name, j, t) if name == "down" else ((name, j, "p"), t)
                    if t == 0 and j == 0:
                        for ss in range(2):
                            for half in range(2):
                                dve.wait_ge(*drained(("gb", n, ss, half)))
                    dve.wait_ge(*filled(label))
                    turn_ = NT * j + t
                    if turn_ >= 2:
                        dve.wait_ge(dve_step, added[turn_ - 2])
                    o = ftmp[:, turn_ % 2, 0:width]
                    v.tensor_tensor(o, bank_of(label)[:, 0:width], GB[:, s, n0:n0 + width], ALU.mult).then_inc(drained(label)[0], 1)
                    dve.wait_ge(*drained(label))
                    x = X[:, t, n0:n0 + width]
                    last = v.tensor_tensor(x, x, o, ALU.add)
                    if final and t == NT - 1:
                        last.then_inc(x_updated, 1)
                    else:
                        added[turn_] = note(last)

            v.memset(raw_a, 0.0).then_inc(raw_zero, 1)
            dve.wait_ge(*filled("col"))
            v.tensor_copy(colT[:, 0, :], bank_of("col")[:, 0:112])
            v.tensor_copy(colT[:, 1, 0:111], bank_of("col")[:, 112:223]).then_inc(drained("col")[0], 1)
            normalise(0)
            dve.wait_ge(*drained("col"))
            add_bias(0)
            modulated(0, 0, 0)
            for ct in range(CCT):
                dve.wait_ge(*drained(("xbc", ct, "p")))
                o = CV[:, ct, :]
                then(v.tensor_scalar(o, raw[:, ct % 4, 0:CVW], convw[:, 0, ct:ct + 1], convb[:, ct:ct + 1], ALU.mult, ALU.add))
                for i in range(1, CW):
                    ins = v.scalar_tensor_tensor(o, raw[:, ct % 4, i:i + CVW], convw[:, i, ct:ct + 1], o, ALU.mult, ALU.add)
                    if i < CW - 1:
                        then(ins)
                    else:
                        ins.then_inc(conv_done, 1)
            dve.wait_ge(small_loaded, 16 * 9)
            dve.wait_ge(*filled("dt"))
            v.tensor_tensor(dtx.rearrange("p (t n) -> p t n", t=NT), bank_of("dt")[:, 0:96].rearrange("p (t n) -> p t n", t=NT),
                            dtb_r.unsqueeze(1).broadcast_to([P, NT, 32]), ALU.add).then_inc(drained("dt")[0], 1)
            dve.wait_ge(*drained("dt"))
            then(v.tensor_scalar(dtw, dtx, -1.0, None, ALU.mult))
            v.tensor_tensor(dtw, dtw, dtx, ALU.min).then_inc(dt_arg, 1)
            dve.wait_ge(dt_exp, 1)
            v.tensor_scalar(dtw, dtu, 1.0, None, ALU.add).then_inc(dt_w, 1)
            dve.wait_ge(dt_ln, 1)
            then(v.tensor_scalar(dtw, dtw, -1.0, None, ALU.add))
            then(v.tensor_scalar(dtA, dtw, 0.0, None, ALU.is_equal))
            then(v.tensor_tensor(dtA, dtA, dtu, ALU.mult))
            then(v.tensor_scalar(dtw, dtw, 2.0 ** -24, None, ALU.max))
            then(v.reciprocal(dtw, dtw))
            then(v.tensor_tensor(dtw, dtw, dtu, ALU.mult))
            then(v.tensor_tensor(dtv, dtv, dtw, ALU.mult))
            then(v.tensor_tensor(dtv, dtv, dtA, ALU.add))
            v.scalar_tensor_tensor(dtt, dtx, 0.0, dtv, ALU.max, ALU.add).then_inc(dt_ready, 1)
            dve.wait_ge(dt_ready, 1)
            dve.wait_ge(dt_exp, 2)
            v.scalar_tensor_tensor(dtA.rearrange("p (t n) -> p t n", t=NT), dtt.rearrange("p (t n) -> p t n", t=NT), -1.0,
                                   aexp.unsqueeze(1).broadcast_to([P, NT, 32]), ALU.mult, ALU.mult).then_inc(dta_ready, 1)
            dve.wait_ge(sq_done, sq_at["v"])
            r = inverse_root("v", NT, D)
            for t in range(NT):
                v.scalar_tensor_tensor(V[:, t, :], V[:, t, :], r[:, t:t + 1], sgn_r, ALU.mult, ALU.mult).then_inc(vn_ready, 1)
            for t in range(NT):
                for half in range(2):
                    label = ("sg", t, half)
                    dve.wait_ge(*filled(label))
                    dve.wait_ge(*drained((("u", half, "p"), t)))
                    for g in range(2):
                        gg = 2 * half + g
                        uu = U[:, t, gg * SGD:(gg + 1) * SGD]
                        last = v.scalar_tensor_tensor(uu, bank_of(label)[:, g * SGD:(g + 1) * SGD], bspc[:, gg:gg + 1], uu, ALU.add, ALU.mult)
                    last.then_inc(drained(label)[0], 1)
            for t in range(NT):
                dve.wait_ge(*filled(("xs", t, 1)))
                v.tensor_copy(XS[:, t, 512:1024], bank_of(("xs", t, 1))[:, :]).then_inc(drained(("xs", t, 1))[0], 1)
            dve.wait_ge(*filled("cs"))
            v.tensor_scalar(csn, bank_of("cs")[:, 0:96], -1.0, None, ALU.mult).then_inc(cs_ready, 1)
            v.tensor_copy(tot, bank_of("cs")[:, 96:192]).then_inc(drained("cs")[0], 1)
            dve.wait_ge(*drained("cs"))
            dve.wait_ge(cs_ready, 1)
            v.tensor_tensor(den, tot, csn, ALU.add).then_inc(end_ready, 1)
            dve.wait_ge(xdt_ready, 6)
            for t in range(NT):
                xs = XS[:, t, :].rearrange("p (h d) -> p h d", h=HEADS)
                then(v.tensor_tensor(xs, xs, dsk_r.unsqueeze(2).broadcast_to([P, HEADS, HD]), ALU.mult))

            def add_state_output(t, d):
                for half in range(2):
                    label = ("off", t, d, half)
                    dve.wait_ge(*filled(label))
                    o = off[:, half, :]
                    e8_ = ecs[:, 32 * t + 16 * d + 8 * half:32 * t + 16 * d + 8 * half + 8]
                    v.tensor_tensor(o.rearrange("p (h d) -> p h d", h=8), bank_of(label)[:, :].rearrange("p (h d) -> p h d", h=8),
                                    e8_.unsqueeze(2).broadcast_to([P, 8, HD]), ALU.mult).then_inc(drained(label)[0], 1)
                    dve.wait_ge(*drained(label))
                    xs = XS[:, t, 512 * half:512 * half + 512]
                    then(v.tensor_tensor(xs, xs, o, ALU.add))

            dve.wait_ge(ex_ready, 3)
            add_state_output(1, 0)
            add_state_output(2, 1)
            for d in range(2):
                dve.wait_ge(*filled(("own", d, 0)))
                dve.wait_ge(*filled(("own", d, 1)))
                s3 = stT[:, d, :].rearrange("p (h d) -> p h d", h=HEADS)
                o = 32 * (1 + d) + 16 * d
                then(v.tensor_tensor(s3, s3, etot[:, o:o + 16].unsqueeze(2).broadcast_to([P, HEADS, HD]), ALU.mult))
                for half in range(2):
                    s2 = stT[:, d, 512 * half:512 * half + 512]
                    v.tensor_tensor(s2, s2, bank_of(("own", d, half))[:, :], ALU.add).then_inc(drained(("own", d, half))[0], 1)
                dve.wait_ge(*drained(("own", d, 0)))
                dve.wait_ge(*drained(("own", d, 1)))
                dve.nop().then_inc(st_upd, 1)
            add_state_output(2, 0)
            add_state_output(1, 1)

            def scan_args(i):
                t, g = TURNS[i]
                if i >= 2:
                    dve.wait_ge(*w_release[i - 2])
                for d in range(2):
                    label = ("cr", i, d)
                    dve.wait_ge(*filled(label))
                    for h in range(HPG):
                        col = 32 * t + 16 * d + HPG * g + h
                        last = v.scalar_tensor_tensor(W[:, i % 2, (4 * d + h) * P:(4 * d + h + 1) * P], bank_of(label)[:, h * P:(h + 1) * P],
                                                      csn[:, col:col + 1], mask[d], ALU.add, ALU.min)
                    last.then_inc(drained(label)[0], 1)
                dve.wait_ge(*drained(("cr", i, 0)))
                dve.wait_ge(*drained(("cr", i, 1)))
                dve.nop().then_inc(arg_ready, 1)

            def add_scan(t, half):
                label = ("y", t, half)
                dve.wait_ge(*filled(label))
                xs = XS[:, t, 512 * half:512 * half + 512]
                v.tensor_tensor(xs, xs, bank_of(label)[:, :], ALU.add).then_inc(drained(label)[0], 1)
                if half == 1:
                    dve.wait_ge(*drained(("y", t, 0)))
                    dve.wait_ge(*drained(label))
                    v.tensor_tensor(XS[:, t, :], XS[:, t, :], Z[:, t, :], ALU.mult).then_inc(y_ready, 1)

            for j in range(2):
                for t in range(NT):
                    dve.wait_ge(*drained((("z", j, "p"), t)))
            scan_args(0)
            for i, (t, g) in enumerate(TURNS):
                if i + 1 < len(TURNS):
                    scan_args(i + 1)
                if g % 2 == 1:
                    add_scan(t, g // 2)
            for t in range(NT):
                dve.wait_ge(sq_done, sq_at[("y", t)])
                r = inverse_root(("y", t), 1, D)
                v.tensor_scalar(XS[:, t, :], XS[:, t, :], r[:, 0:1], None, ALU.mult).then_inc(yn_ready, 1)
            for t in range(NT):
                label = ("yy", t, 1)
                dve.wait_ge(*filled(label))
                for k in range(4, 8):
                    last = v.tensor_scalar(YT[:, k, t * P:(t + 1) * P], bank_of(label)[:, (k - 4) * P:(k - 3) * P], ssdn[:, k:k + 1], None, ALU.mult)
                last.then_inc(drained(label)[0], 1)
            for j in range(4):
                gated_update("wout", j, 256 * j, 256, j == 3, 0)
            dve.wait_ge(x_updated, 1)
            normalise(1)
            modulated(1, 0, 3)

            for f in range(FT):
                dve.wait_ge(*drained(("g", f)))
                dve.wait_ge(*filled(("u", f)))
                v.tensor_tensor(aT[:, f, :], sg[:, f % 2, :], bank_of(("u", f))[:, 0:TOK], ALU.mult).then_inc(drained(("u", f))[0], 1)
            for dp in range(4):
                gated_update("down", dp, 256 * dp, 256, dp == 3, 1)

            dve.wait_ge(x_updated, 2)
            normalise(2)
            add_bias(1)
            modulated(2, 1, 0)
            dve.wait_ge(sq_done, sq_at["qa"])
            r = inverse_root("qa", NT, QR)
            for t in range(NT):
                v.tensor_scalar(qa[:, t, :], qa[:, t, :], r[:, t:t + 1], None, ALU.mult).then_inc(qa_ready, 1)
            dve.wait_ge(sq_done, sq_at["ckv"])
            r = inverse_root("ckv", NT, KVR)
            for t in range(NT):
                v.scalar_tensor_tensor(ckv[:, t, :], ckv[:, t, :], r[:, t:t + 1], kvn_r, ALU.mult, ALU.mult).then_inc(ckv_ready, 1)

            def head_norm(i):
                kind, t = TILES[i]
                b = i % 2
                i_root, cols = root_at(("kq", i))
                dve.wait_ge(sq_done, sq_at[("kq", i)])
                then(v.tensor_reduce(cols, junk[:, 0:D].rearrange("p (h n) -> p h n", h=MH), AXX, ALU.add))
                hr = small[:, 256:264]
                then(v.tensor_reduce(hr, junk[:, D:].rearrange("p (h n) -> p h n", h=MH), AXX, ALU.add))
                then(v.tensor_tensor(cols, cols, hr, ALU.add))
                r = inverse_root(("kq", i), MH, QK)
                gain = kn_r if kind == "k" else qn_r
                for h in range(MH):
                    kn_, kr_ = KQN[:, b, h, :], KQR[:, b, h, :]
                    v.scalar_tensor_tensor(kn_, kn_, r[:, h:h + 1], gain[:, 0:NOPE], ALU.mult, ALU.mult)
                    last = v.scalar_tensor_tensor(kr_, kr_, r[:, h:h + 1], gain[:, NOPE:], ALU.mult, ALU.mult)
                if t not in (1, 2):
                    last.then_inc(kq_ready, 1)
                    return
                then(last)
                pe_ = KQR[:, b, :, :].rearrange("p h (a f m) -> p h a f m", a=2, f=2)
                x1, x2 = pe_[:, :, :, 0, :], pe_[:, :, :, 1, :]
                co = cosT[t - 1].unsqueeze(1).broadcast_to([P, MH, 2, 16])
                si = sinT[t - 1].unsqueeze(1).broadcast_to([P, MH, 2, 16])
                v.tensor_tensor(rt[:, 0], x1, co, ALU.mult)
                v.tensor_tensor(rt[:, 1], x2, si, ALU.mult)
                v.tensor_tensor(rt[:, 2], x1, si, ALU.mult)
                then(v.tensor_tensor(rt[:, 3], x2, co, ALU.mult))
                v.tensor_tensor(x1, rt[:, 0], rt[:, 1], ALU.subtract)
                v.tensor_tensor(x2, rt[:, 2], rt[:, 3], ALU.add).then_inc(kq_ready, 1)

            def turned(i):
                kind, t = TILES[i]
                n_to = kTn if kind == "k" else qTn
                label = ("hT", i, 1)
                dve.wait_ge(*filled(label))
                v.tensor_copy(n_to[:, 4:8, t * P:(t + 1) * P], bank_of(label)[:, :].rearrange("p (k t) -> p k t", k=4)).then_inc(drained(label)[0], 1)

            for i in range(len(TILES)):
                head_norm(i)
                if i > 0:
                    turned(i - 1)
            turned(len(TILES) - 1)

            def maximum(n):
                h, t = HEAD_TILES[n]
                kn = P if t == 0 else TOK
                dve.wait_ge(*filled(("s", n)))
                then(v.reduce_max(nmx[:, n:n + 1], bank_of(("s", n))[:, 0:kn], AXX))
                v.tensor_scalar(nmx[:, n:n + 1], nmx[:, n:n + 1], -QK ** -0.5, None, ALU.mult).then_inc(mx_ready, 1)

            def head_out(h):
                dve.wait_ge(*filled(("o", h)))
                v.tensor_copy(OT[:, h, :], bank_of(("o", h))[:, 0:TOK]).then_inc(drained(("o", h))[0], 1)

            maximum(0)
            for n, (h, t) in enumerate(HEAD_TILES):
                kn = P if t == 0 else TOK
                if n + 1 < len(HEAD_TILES):
                    maximum(n + 1)
                dve.wait_ge(*drained(("s", n)))
                then(v.reciprocal(psum_[:, n:n + 1], psum_[:, n:n + 1]))
                pr = PR[:, n % 2, 0:kn]
                v.tensor_scalar(pr, pr, psum_[:, n:n + 1], None, ALU.mult).then_inc(pr_ready, 1)
                if t == 1 and h > 0:
                    head_out(h - 1)
            head_out(MH - 1)
            for j, (n0, w_) in enumerate(WO_COLS):
                gated_update("wo", j, n0, w_, j == len(WO_COLS) - 1, 2)

            v.memset(yT_a, 0.0).then_inc(moe_zero, 1)
            v.memset(PGT[:, :, :], 0.0).then_inc(moe_zero, 1)
            v.memset(YA[:, :, :], 0.0).then_inc(moe_zero, 1)
            dve.wait_ge(x_updated, 3)
            normalise(3)
            modulated(3, 1, 3)
            dve.wait_ge(iota_loaded, 16)
            dve.wait_ge(*filled("lg"))
            v.tensor_copy(lg, bank_of("lg")[:, 0:24].rearrange("p (t e) -> p t e", t=NT)).then_inc(drained("lg")[0], 1)
            dve.wait_ge(*drained("lg"))
            for t in range(NT):
                then(v.max(top[:, t, :], lg[:, t, :]))
                then(v.max_index(idxu[:, t, :], top[:, t, :], lg[:, t, :]))
            then(v.tensor_copy(idxf, idxu[:, :, :]))
            for t in range(NT):
                v.tensor_scalar(oh1[:, t, :], iota[:, 0:8], idxf[:, t, 0:1], None, ALU.is_equal)
                then(v.tensor_scalar(sel[:, t, :], iota[:, 0:8], idxf[:, t, 1:2], None, ALU.is_equal))
            v.tensor_tensor(gpair[:, 0:3], top[:, :, 1], top[:, :, 0], ALU.subtract).then_inc(ex8_arg, 1)
            dve.wait_ge(ex8_ready, 1)
            then(v.tensor_scalar(gpair[:, 3:6], gpair[:, 0:3], 1.0, None, ALU.add))
            then(v.reciprocal(gpair[:, 3:6], gpair[:, 3:6]))
            then(v.tensor_tensor(gpair[:, 6:9], gpair[:, 0:3], gpair[:, 3:6], ALU.mult))
            then(v.memset(gate, 0.0))
            for t in range(NT):
                then(v.tensor_scalar(gate[:, t, 0:8], sel[:, t, :], gpair[:, 6 + t:7 + t], None, ALU.mult))
                then(v.scalar_tensor_tensor(gate[:, t, 0:8], oh1[:, t, :], gpair[:, 3 + t:4 + t], gate[:, t, 0:8], ALU.mult, ALU.add))
            v.tensor_tensor(sel, sel, oh1, ALU.add).then_inc(sel_ready, 1)
            dve.wait_ge(sel_ready, 1)
            then(v.memset(rank, -1.0))
            dve.wait_ge(*filled("rank"))
            then(v.scalar_tensor_tensor(rank[:, :, 0:8], bank_of("rank")[:, 0:24].rearrange("p (t e) -> p t e", t=NT), 1.0, sel, ALU.add, ALU.mult))
            then(v.tensor_scalar(rank[:, :, 0:8], rank[:, :, 0:8], -1.0, None, ALU.add))
            v.tensor_copy(cnt, bank_of("rank")[:, 24:32]).then_inc(drained("rank")[0], 1)
            dve.wait_ge(*drained("rank"))

            def slots(e, out, gated):
                for t in range(NT):
                    last = v.tensor_scalar(out[:, t, :], iota, rank[:, t, bass.ds(e, 1)] if not isinstance(e, int) else rank[:, t, e:e + 1],
                                           gate[:, t, bass.ds(e, 1)] if gated else None, ALU.is_equal, *([ALU.mult] if gated else []))
                return last

            slots(0, PS, False).then_inc(ps_ready, 1)
            then(v.memset(vsum, 0.0))
            for w_ in WIDTHS[:-1]:
                then(v.scalar_tensor_tensor(vsum[:, 1:9], cnt, float(w_), vsum[:, 1:9], ALU.is_gt, ALU.add))
            then(v.tensor_copy(vtab[:, 0, :], vsum))
            then(v.memset(vsum, 1.0))
            for w_ in (P, 2 * P):
                then(v.scalar_tensor_tensor(vsum[:, 1:9], cnt, float(w_), vsum[:, 1:9], ALU.is_gt, ALU.add))
            v.tensor_copy(vtab[:, 1, :], vsum).then_inc(route_ready, 1)
            for t in range(NT):
                dve.wait_ge(*filled(("h2", t, 1)))
                v.tensor_copy(H2[:, t, 512:1024], bank_of(("h2", t, 1))[:, :]).then_inc(drained(("h2", t, 1))[0], 1)
            dve.wait_ge(*filled(("ga0", KT - 1)))

            def moe_bank_of(label):
                return PSUM[place[("moe",) + label][0]]

            with dve.Fori(0, NE) as e:
                for i in (1, 3, 5):
                    dve.wait_ge(*moe_filled(("T", i), e))
                    v.tensor_copy(yt[:, i // 2, 512:1024], moe_bank_of(("T", i))[:, :]).then_inc(moe_drained(("T", i), e)[0], 1)
                slots(e + 1, PS, False).then_inc(ps_ready, 1)
                slots(e, PG, True).then_inc(pg_ready, 1)
                for f in range(FT):
                    dve.wait_ge(*moe_drained(("g", f), e))
                    dve.wait_ge(*moe_filled(("u", f), e))
                    v.tensor_tensor(aT[:, f, :], sg[:, f % 2, :], moe_bank_of(("u", f))[:, 0:TOK], ALU.mult).then_inc(moe_drained(("u", f), e)[0], 1)
                for i in range(6):
                    dve.wait_ge(*moe_filled(("sc", i), e))
                    ya = YA[:, i // 2, 512 * (i % 2):512 * (i % 2) + 512]
                    v.tensor_tensor(ya, ya, moe_bank_of(("sc", i))[:, :], ALU.add).then_inc(moe_drained(("sc", i), e)[0], 1)
                for k in (0, 2, 4, 6):
                    dve.wait_ge(*moe_filled(("dn", k), e))
                    v.tensor_copy(yT[:, k, :], moe_bank_of(("dn", k))[:, 0:TOK]).then_inc(moe_drained(("dn", k), e)[0], 1)
            for i in (1, 3, 5):
                dve.wait_ge(*filled(("lastT", i)))
                v.tensor_copy(yt[:, i // 2, 512:1024], bank_of(("lastT", i))[:, :]).then_inc(drained(("lastT", i))[0], 1)
            for s in range(2):
                for half in range(2):
                    dve.wait_ge(*drained(("gb", 3, s, half)))
            for i in range(6):
                t, half = i // 2, i % 2
                label = ("last", i)
                dve.wait_ge(*filled(label))
                ya = YA[:, t, 512 * half:512 * half + 512]
                v.tensor_tensor(ya, ya, bank_of(label)[:, :], ALU.add).then_inc(drained(label)[0], 1)
                dve.wait_ge(*drained(label))
                then(v.tensor_tensor(ya, ya, GB[:, 0 if t == 0 else 1, 512 * half:512 * half + 512], ALU.mult))
                x = X[:, t, 512 * half:512 * half + 512]
                v.tensor_tensor(x, x, ya, ALU.add).then_inc(x_updated, 1)

        @block.gpsimd
        def _(pool):
            g_ = nc.gpsimd

            def by_head(a):
                return a.rearrange("p (h d) -> p h d", h=HEADS)

            def over(a):
                return a.unsqueeze(2).broadcast_to([P, HEADS, HD])

            pool.wait_ge(dt_ready, 1)
            pool.wait_ge(*filled((("z", 1, "p"), NT - 1)))
            for t in range(NT):
                pool.wait_ge(*drained(("xs", t, 0)))
                pool.wait_ge(*drained(("xs", t, 1)))
                for d in range(2):
                    o = 32 * t + 16 * d
                    g_.tensor_tensor(by_head(xdt[:, t, d, :]), by_head(XS[:, t, :]), over(dtt[:, o:o + 16]), ALU.mult).then_inc(xdt_ready, 1)
            pool.wait_ge(ex_ready, 2)
            pool.wait_ge(*filled(("st", 1, 1)))
            pool.wait_ge(xdt_ready, 6)
            for n, (t, d) in enumerate(((0, 0), (0, 1), (1, 0), (2, 1))):
                if n >= 2:
                    pool.wait_ge(*filled(("cst", d, 1)))
                o = 32 * t + 16 * d
                g_.tensor_tensor(by_head(W[:, d, :]), by_head(xdt[:, t, d, :]), over(den[:, o:o + 16]), ALU.mult).then_inc(xde_ready, 1)
            for t in range(NT):
                pool.wait_ge(*drained(("cb", t)))
            for i, (t, g) in enumerate(TURNS):
                pool.wait_ge(exp_ready, i + 1)
                w8 = W[:, i % 2, :].rearrange("p (h l) -> p h l", h=8)
                g_.tensor_tensor(w8, w8, cb[:, t, g, :].unsqueeze(1).broadcast_to([P, 8, P]), ALU.mult).then_inc(wm_ready, 1)

        @block.sync
        def _(sp):
            def load(n):
                label, parts = chunks[n]
                s = n % RING
                if n >= RING:
                    sp.wait_ge(*released[chunks[n - RING][0]])
                for at, src in parts:
                    k, w = src.shape[1], src.shape[2]
                    sp.dma_start(ring[:, s, at:at + k * w].rearrange("p (k n) -> p k n", k=k), src).then_inc(ring_full[s], 16)

            sp.dma_start(X[:, 0, :], x_prompt[0]).then_inc(x_loaded, 16)
            sp.dma_start(X[:, 1:3, :], x_sample[0].rearrange("(t p) d -> p t d", p=P)).then_inc(x_loaded, 16)
            first_v = [l for l, _ in chunks].index(("v", 0))
            for n in range(first_v):
                load(n)
            sp.wait_ge(*filled("wsp"))
            sp.dma_start(st_raw, state_ssm[0, 0].rearrange("d (i hh) q n -> (hh q) d i n", hh=2)).then_inc(st_loaded, 16)
            first_wout = [l for l, _ in chunks].index(("wout", 2))
            for n in range(first_v, first_wout):
                load(n)
            for d in range(2):
                sp.wait_ge(*drained(("cst", d, 0)))
                sp.wait_ge(*drained(("cst", d, 1)))
                sp.dma_start(new_state[0, 0, d].rearrange("(i hh) q n -> (hh q) i n", hh=2), cst[:, d, :, :]).then_inc(state_out, 16)
            first_dq = [l for l, _ in chunks].index("dq")
            for n in range(first_wout, first_dq):
                load(n)
            sp.wait_ge(x_updated, 2)
            sp.dma_start(ckv[:, 3, :], cache_ckv[0, 0]).then_inc(cache_loaded, 16)
            sp.dma_start(kpe[:, 3, :], cache_kpe[0, 0]).then_inc(cache_loaded, 16)
            for n in range(first_dq, first_dq + 3):
                load(n)
            sp.wait_ge(ckv_ready, 3)
            sp.dma_start(new_ckv[0, 0], ckv[:, 0, :]).then_inc(kv_out, 16)
            sp.dma_start(new_kpe[0, 0], kpe[:, 0, :]).then_inc(kv_out, 16)
            for n in range(first_dq + 3, STATIC):
                load(n)

            def moe_released(i, e):
                label = MOE_CHUNKS[i]
                if label[1] == "gu":
                    f0, n = GU[label[2]]
                    return moe_filled(("u", f0 + n - 1), e)
                _, _, dp, fh = label
                if fh == 1:
                    return moe_filled(("dn", 2 * dp + 1), e)
                return chunk_used, e * 4 + (used_before_moe[0] + dp + 1)

            def moe_parts(i, e):
                label = MOE_CHUNKS[i]
                if label[1] == "gu":
                    f0, n = GU[label[2]]
                    for at, wgt in ((0, moe_w_gate), (2048, moe_w_up)):
                        yield at, wgt[0, bass.ds(e, 1), :, P * f0:P * (f0 + n)].rearrange("a (k p) n -> p (a k) n", p=P)
                else:
                    _, _, dp, fh = label
                    yield 0, moe_w_down[0, bass.ds(e, 1), FH * P * fh:FH * P * (fh + 1), 256 * dp:256 * dp + 256].rearrange("a (k p) n -> p (a k) n", p=P)

            def moe_load(i, e):
                s = i % RING
                for at, src in moe_parts(i, e):
                    k, w = src.shape[1], src.shape[2]
                    sp.dma_start(ring[:, s, at:at + k * w].rearrange("p (k n) -> p k n", k=k), src).then_inc(ring_full[s], 16)

            for i in range(RING):
                sp.wait_ge(*released[chunks[STATIC - RING + i][0]])
                moe_load(i, 0)
            sp.wait_ge(x_updated, 3)
            sp.dma_start(iota, iota_dram).then_inc(iota_loaded, 16)
            with sp.Fori(0, NE - 1) as e:
                for i in range(len(MOE_CHUNKS)):
                    sp.wait_ge(*moe_released(i, e))
                    j = i + RING
                    if MOE_CHUNKS[j % len(MOE_CHUNKS)] == ("moe", "dn", 0, 0):
                        sp.sem_inc(down_begun, 1)
                    moe_load(j % len(MOE_CHUNKS), e + j // len(MOE_CHUNKS))
            for i in range(len(MOE_CHUNKS) - RING):
                sp.wait_ge(*moe_released(i, NE - 1))
                moe_load(i + RING, NE - 1)
            for t in range(NT):
                sp.wait_ge(x_updated, 3 + 2 * (t + 1))
                dst = y_prompt[0] if t == 0 else y_sample[0, (t - 1) * P:t * P, :]
                sp.dma_start(dst, X[:, t, :]).then_inc(y_out, 16)
            sp.wait_ge(state_out, 32)
            sp.wait_ge(kv_out, 32)
            sp.wait_ge(y_out, 48)


_INS = ['x_prompt', 'x_sample', 'c', 'state_ssm', 'cache_ckv', 'cache_kpe', 'c_ctx', 'w_mod', 'b_mod',
        'w_in', 'conv_w', 'conv_b', 'dt_bias', 'a_log', 'd_skip', 'ssd_norm', 'sgu_norm', 'w_sp', 'b_sp', 'w_out',
        'ffn_w_gate', 'ffn_w_up', 'ffn_w_down', 'w_dq', 'q_a_norm', 'w_uq', 'w_dkv', 'kv_a_norm', 'w_ukv',
        'q_norm', 'k_norm', 'w_o', 'router', 'moe_w_gate', 'moe_w_up', 'moe_w_down']
_OUTS = [((1, 128, 1024), 'float32'), ((1, 256, 1024), 'float32'), ((1, 1, 2, 16, 64, 128), 'float32'),
         ((1, 1, 128, 256), 'float32'), ((1, 1, 128, 64), 'float32')]


def kernel(**inputs):
    import numpy as _np
    import concourse.bacc as _bacc
    from concourse import mybir as _mybir
    from concourse.bass_utils import run_bass_kernel_spmd as _run

    nc = _bacc.Bacc("TRN2", target_bir_lowering=False, num_devices=1, dynamic_dma_scratch_size=1024)
    arrays, args = {}, []
    for name in _INS:
        a = _np.ascontiguousarray(inputs[name])
        arrays[f"in_{name}_dram"] = a
        args.append(nc.dram_tensor(f"in_{name}_dram", a.shape, _mybir.dt.from_np(a.dtype), kind="ExternalInput").ap())
    for i, (shape, dtype) in enumerate(_OUTS):
        dt = _mybir.dt.from_np(_np.dtype(dtype))
        args.append(nc.dram_tensor(f"out_{i}_dram", shape, dt, kind="ExternalOutput").ap())
    hybrid_trunk(nc, *args)
    r = _run(nc, [arrays], core_ids=[0])
    return tuple(r.results[0][f"out_{i}_dram"] for i in range(len(_OUTS)))
```

```python
from contextlib import ExitStack

import numpy as np
import concourse.bass as bass
from concourse import mybir

F32 = mybir.dt.float32
I32 = mybir.dt.int32
U32 = mybir.dt.uint32
ACT = mybir.ActivationFunctionType
ALU = mybir.AluOpType
AXX = mybir.AxisListType.X

P = 128
D = 1024
KT = D // P
NT = 3
TOK = NT * P
LAT = 2 * P
EPS = 1e-6
NMOD = 6 * KT
HEADS, HD, GROUPS, STATE = 16, 64, 4, 128
HPG = HEADS // GROUPS
CCT = 16
CW = 5
PAD = CW // 2
RAW = PAD + P + PAD + LAT + PAD
CVW = RAW - 2 * PAD
TOK0 = [0, P + PAD, 2 * P + PAD]
SGRP, SGD = 4, 256
MH, QR, KVR, NOPE, ROPE, VH = 8, 384, 256, 128, 64, 128
QK = NOPE + ROPE
KTILES = 4
FF = 2816
FT = FF // P
NE = 8
GRID_W = 64
RING = 4
SLOT = 4096
BANKS = 8
NEG = -1e30
WIDTHS = [64, 128, 160, 192, 256, 384]
NARROW = 64
GU = [(2 * j, 2) for j in range(10)] + [(20, 1), (21, 1)]
GU_LAST = [f0 + n - 1 for f0, n in GU]
DN = [(dp, fh) for dp in range(4) for fh in range(2)]
FH = FT // 2


def constants():
    i = np.arange(P)
    upper = (i[:, None] <= i[None, :]).astype(np.float32)
    lower = (i[:, None] >= i[None, :]).astype(np.float32)
    eye = np.eye(P, dtype=np.float32)
    inv = (np.float32(10000.0) ** (-np.arange(0, ROPE // 2, 2, dtype=np.float32) / np.float32(ROPE // 2))).astype(np.float32)
    fold = np.zeros((P, P), np.float32)
    fold[i, i % NARROW] = 1.0
    tabs = []
    for tile in range(2):
        tok = tile * P + i
        ang = np.stack([(tok // GRID_W).astype(np.float32)[:, None] * inv,
                        (tok % GRID_W).astype(np.float32)[:, None] * inv], axis=1)
        tabs += [np.cos(ang).reshape(P, 32), np.sin(ang).reshape(P, 32)]
    return np.concatenate([eye, upper, lower, np.ones((P, P), np.float32),
                           np.where(upper > 0, 0.0, NEG), np.where(lower > 0, 0.0, NEG), upper - eye]
                          + tabs + [np.stack([(i % 32 == s) for s in range(2)], axis=1).astype(np.float32), fold],
                          axis=1).astype(np.float32)


def hybrid_trunk(nc, x_prompt, x_sample, c, state_ssm, cache_ckv, cache_kpe, c_ctx, w_mod, b_mod,
                 w_in, conv_w, conv_b, dt_bias, a_log, d_skip, ssd_norm, sgu_norm, w_sp, b_sp, w_out,
                 ffn_w_gate, ffn_w_up, ffn_w_down, w_dq, q_a_norm, w_uq, w_dkv, kv_a_norm, w_ukv,
                 q_norm, k_norm, w_o, router, moe_w_gate, moe_w_up, moe_w_down,
                 y_prompt, y_sample, new_state, new_ckv, new_kpe):
    ctx = ExitStack()
    with ctx:
        def sb(name, shape, dt=F32):
            return ctx.enter_context(nc.sbuf_tensor(name, shape, dt))

        def sem(name):
            return ctx.enter_context(nc.semaphore(name))

        ring = sb("ring", [P, RING, SLOT])
        X = sb("X", [P, NT, D])
        HTXN = sb("HTXN", [P, 2 * KT * TOK])
        HT = HTXN[:, 0:KT * TOK].rearrange("p (k t) -> p k t", k=KT)
        XN = HTXN[:, KT * TOK:].rearrange("p (t d) -> p t d", t=NT)
        consts_np = constants()
        CST = sb("CST", [P, consts_np.shape[1]])
        ident, upper, lower, ones = (CST[:, n * P:(n + 1) * P] for n in range(4))
        mask = [CST[:, 4 * P:5 * P], CST[:, 5 * P:6 * P]]
        before = CST[:, 6 * P:7 * P]
        cosT = [CST[:, 7 * P + 64 * i:7 * P + 64 * i + 32].rearrange("p (a m) -> p a m", a=2) for i in range(2)]
        sinT = [CST[:, 7 * P + 64 * i + 32:7 * P + 64 * i + 64].rearrange("p (a m) -> p a m", a=2) for i in range(2)]
        pick = CST[:, 7 * P + 128:7 * P + 130]
        fold = CST[:, 7 * P + 130:8 * P + 130]
        tri = [upper, lower]
        colT = sb("colT", [P, 2, 112])
        modT = sb("modT", [P, 2, NMOD, 2])
        mrow = sb("mrow", [P, 2, 512])
        GB = sb("GB", [P, 2, D])
        rows = sb("rows", [P, 32 + 32 + 16 + 2 * QK + KVR])
        dtb_r, alog_r, dsk_r = rows[:, 0:32], rows[:, 32:64], rows[:, 64:80]
        qn_r, kn_r, kvn_r = rows[:, 80:80 + QK], rows[:, 80 + QK:80 + 2 * QK], rows[:, 80 + 2 * QK:]
        wdt = sb("wdt", [P, KT, 32])
        wrt = sb("wrt", [P, KT, NE])
        wspT = sb("wspT", [P, SGRP, P])
        stat = sb("stat", [P, 256])
        sv = sb("sv", [P, 2, KT])
        bmodc = colT[:, 0, 16:112].rearrange("p (l m) -> p l m", l=2)
        convw = colT[:, 1, 0:80].rearrange("p (i c) -> p i c", i=CW)
        convb, ssdn, bspc, qanc = colT[:, 1, 80:96], colT[:, 1, 96:104], colT[:, 1, 104:108], colT[:, 1, 108:111]

        ARENA = 22100
        arena = sb("arena", [P, ARENA])

        def lay(sizes):
            out, at = [], 0
            for n in sizes:
                out.append(arena[:, at:at + n])
                at += n
            assert at <= ARENA, at
            return out

        cv_a, raw_a, z_a, u_a, v_a, bt_a, w_a, sgn_r = lay([CCT * CVW, 4 * RAW, NT * D, NT * D, NT * D, NT * 512, 2048, D])
        CV = cv_a.rearrange("p (c t) -> p c t", c=CCT)
        raw = raw_a.rearrange("p (b t) -> p b t", b=4)
        cb = raw_a[:, 0:NT * 512].rearrange("p (c g l) -> p c g l", c=NT, g=GROUPS)
        Z, U, V = (a.rearrange("p (t d) -> p t d", t=NT) for a in (z_a, u_a, v_a))
        XS = V
        BT = bt_a.rearrange("p (t n) -> p t n", t=NT)
        W = w_a.rearrange("p (b n) -> p b n", b=2)
        praw = w_a[:, 0:6 * P].rearrange("p (r n) -> p r n", r=6)
        st_raw = w_a.rearrange("p (d i n) -> p d i n", d=2, i=KT)
        stT = GB
        xdt = HTXN[:, 0:6 * D].rearrange("p (c d n) -> p c d n", c=NT, d=2)
        cst = cv_a[:, 0:2048].rearrange("p (d i n) -> p d i n", d=2, i=KT)
        off = cv_a[:, 2048:3072].rearrange("p (b n) -> p b n", b=2)
        YT = cv_a[:, 0:2 * KT * TOK].rearrange("p (k t) -> p k t", k=2 * KT)
        aT_a, sg_a, tmp_a = lay([FT * TOK, 2 * TOK, 1024])
        aT = aT_a.rearrange("p (f t) -> p f t", f=FT)
        sg = sg_a.rearrange("p (b t) -> p b t", b=2)
        ftmp = tmp_a.rearrange("p (b n) -> p b n", b=2)
        (v4_a, kt_a, kp_a, qt_a, qp_a, kq_a, ckvT_a, ckv_a, kpe_a, qaT_a) = lay(
            [KTILES * D, MH * 512, 4 * 512, MH * TOK, 4 * TOK, 2 * MH * QK, 2 * 512, KTILES * KVR, KTILES * ROPE, 3 * TOK])
        VV = v4_a.rearrange("p (k n) -> p k n", k=KTILES)
        kTn = kt_a.rearrange("p (h t) -> p h t", h=MH)
        kTr = kp_a.rearrange("p (h t) -> p h t", h=4)
        qTn = qt_a.rearrange("p (h t) -> p h t", h=MH)
        qTr = qp_a.rearrange("p (h t) -> p h t", h=4)
        kq_v = kq_a.rearrange("p (b n) -> p b n", b=2)
        KQN = kq_v[:, :, 0:D].rearrange("p b (h n) -> p b h n", h=MH)
        KQR = kq_v[:, :, D:].rearrange("p b (h n) -> p b h n", h=MH)
        ckvT = ckvT_a.rearrange("p (k t) -> p k t", k=2)
        ckv = ckv_a.rearrange("p (k n) -> p k n", k=KTILES)
        kpe = kpe_a.rearrange("p (k n) -> p k n", k=KTILES)
        qaT = qaT_a.rearrange("p (k t) -> p k t", k=3)
        xn_a = HTXN[:, KT * TOK:]
        qa = xn_a[:, 0:3 * QR].rearrange("p (t n) -> p t n", t=NT)
        junk = xn_a[:, 1152:1152 + MH * QK]
        rt = xn_a[:, 1152:1152 + 1024].rearrange("p (b h a m) -> p b h a m", b=4, h=MH, a=2)
        PR = kq_a[:, 0:4 * TOK].rearrange("p (b n) -> p b n", b=4)
        PT = xn_a[:, 768:768 + 2 * 896].rearrange("p (b n) -> p b n", b=2)
        OT = HT
        (_, _, _, yT_a, yt_a, pg_a, pgT_a, yac_a) = lay(
            [FT * TOK, 2 * TOK, 1024, KT * TOK, NT * D, NT * TOK, NT * TOK, NT * D])
        halves = tmp_a.rearrange("p (b n) -> p b n", b=2)
        H2 = XN
        xeT = HT
        yT = yT_a.rearrange("p (k t) -> p k t", k=KT)
        yt = yt_a.rearrange("p (s d) -> p s d", s=NT)
        PG = pg_a.rearrange("p (t s) -> p t s", t=NT)
        PGT = pgT_a.rearrange("p (s t) -> p s t", s=NT)
        YA = yac_a.rearrange("p (t d) -> p t d", t=NT)
        gb_a = GB[:, :, :].rearrange("p s d -> p (s d)")
        PS = gb_a[:, 0:NT * TOK].rearrange("p (t s) -> p t s", t=NT)
        iota = gb_a[:, 1152:1152 + TOK]
        small = sb("small", [P, 8 * 96])
        dtx, dtu, dtw, dtv, dtA, csn, tot, ecs = (small[:, 96 * n:96 * (n + 1)] for n in range(8))
        den = dtw
        etot = dtv
        small2 = sb("small2", [P, 32 + 96])
        aexp, dtt = small2[:, 0:32], small2[:, 32:128]
        lg = small[:, 0:24].rearrange("p (t e) -> p t e", t=NT)
        top = small[:, 24:48].rearrange("p (t e) -> p t e", t=NT)
        idxf = small[:, 48:72].rearrange("p (t e) -> p t e", t=NT)
        oh1 = small[:, 96:120].rearrange("p (t e) -> p t e", t=NT)
        sel = small[:, 120:144].rearrange("p (t e) -> p t e", t=NT)
        rank = small[:, 144:171].rearrange("p (t e) -> p t e", t=NT)
        gate = small[:, 176:203].rearrange("p (t e) -> p t e", t=NT)
        gpair = small[:, 208:220]
        cnt = small[:, 224:232]
        vsum = small[:, 232:242]
        e8 = small[:, 244:252]
        idxu = sb("idxu", [P, NT, 8], U32)
        vtab = sb("vtab", [P, 2, 10], I32)
        nmx, psum_ = stat[:, 200:224], stat[:, 224:248]

        PSUM = [ctx.enter_context(nc.psum_tensor(f"bank{b}", [P, 512], F32)) for b in range(BANKS)]

        def sems(*names):
            return [sem(n) for n in names]

        ring_full = [sem(f"ring_full{s}") for s in range(RING)]
        bank_full = [sem(f"bank_full{b}") for b in range(BANKS)]
        bank_free = [sem(f"bank_free{b}") for b in range(BANKS)]
        chunk_used, w_used = sems("chunk_used", "w_used")
        x_loaded, const_loaded, small_loaded, prow_loaded, wsp_loaded, st_loaded, cache_loaded, iota_loaded = sems(
            "x_loaded", "const_loaded", "small_loaded", "prow_loaded", "wsp_loaded", "st_loaded", "cache_loaded", "iota_loaded")
        banks_zero, down_begun = sems("banks_zero", "down_begun")
        state_out, kv_out, y_out = sems("state_out", "kv_out", "y_out")
        dve_step, = sems("dve_step")
        sq_done, ms_ready, rt_ready = sems("sq_done", "ms_ready", "rt_ready")
        xn_ready, x_updated, mod_ready, sv_ready = sems("xn_ready", "x_updated", "mod_ready", "sv_ready")
        raw_zero, conv_done, cv_ready, vn_ready = sems("raw_zero", "conv_done", "cv_ready", "vn_ready")
        dt_arg, dt_exp, dt_w, dt_ln, dt_ready, dta_ready = sems("dt_arg", "dt_exp", "dt_w", "dt_ln", "dt_ready", "dta_ready")
        cs_ready, end_ready, ex_ready = sems("cs_ready", "end_ready", "ex_ready")
        xdt_ready, xde_ready, st_upd = sems("xdt_ready", "xde_ready", "st_upd")
        arg_ready, exp_ready, wm_ready, y_ready, yn_ready = sems("arg_ready", "exp_ready", "wm_ready", "y_ready", "yn_ready")
        qa_ready, ckv_ready, kq_ready, kpe_ready = sems("qa_ready", "ckv_ready", "kq_ready", "kpe_ready")
        mx_ready, pr_ready = sems("mx_ready", "pr_ready")
        ex8_arg, ex8_ready, sel_ready, route_ready = sems("ex8_arg", "ex8_ready", "sel_ready", "route_ready")
        moe_zero, ps_ready, pg_ready = sems("moe_zero", "ps_ready", "pg_ready")
        halves_full, halves_copied = sems("halves_full", "halves_copied")

        MOD_WITH = {"v": 8, "u": 10}
        def kmaj(w):
            return w.rearrange("(k p) n -> p k n", p=P)

        chunks, where, released = [], {}, {}
        full_at = [0] * RING

        def chunk(label, *parts):
            s = len(chunks) % RING
            full_at[s] += 16 * len(parts)
            where[label] = (s, full_at[s])
            chunks.append((label, parts))

        def mod_chunk(layer, j):
            chunk(("mod", layer, j), (0, kmaj(w_mod[layer])[:, :, 512 * j:512 * j + 512]))

        def ff_chunks(label, wg, wu, wd):
            for j, (f0, n) in enumerate(GU):
                chunk((label, "gu", j), (0, kmaj(wg)[:, :, P * f0:P * (f0 + n)]),
                      (2048, kmaj(wu)[:, :, P * f0:P * (f0 + n)]))
                if label == "ffn":
                    mod_chunk(1, j)
            for dp, fh in DN:
                chunk((label, "dn", dp, fh), (0, kmaj(wd)[:, FH * fh:FH * (fh + 1), 256 * dp:256 * dp + 256]))

        win = kmaj(w_in[0])
        for j in range(4):
            mod_chunk(0, j)
        for j in range(4):
            chunk(("xbc", j), (0, win[:, :, D + 512 * j:D + 512 * j + 512]))
            mod_chunk(0, 4 + j)
        V0 = D + 2048 + 32 + D
        for name, c0 in (("v", V0), ("u", V0 - D), ("z", 0)):
            for j in range(2):
                chunk((name, j), (0, win[:, :, c0 + 512 * j:c0 + 512 * j + 512]))
                if name != "z":
                    mod_chunk(0, MOD_WITH[name] + j)
        for j in range(4):
            chunk(("wout", j), (0, kmaj(w_out[0])[:, :, 256 * j:256 * j + 256]))
        ff_chunks("ffn", ffn_w_gate[0], ffn_w_up[0], ffn_w_down[0])
        chunk("dq", (0, kmaj(w_dq[0])))
        chunk("dkv", (0, kmaj(w_dkv[0])))
        chunk("ukv", (0, kmaj(w_ukv[0])))
        for j in range(2):
            chunk(("uq", j), (0, kmaj(w_uq[0])[:, :, 768 * j:768 * j + 768]))
        WO_PARTS = 2 + (-(len(chunks) + 2)) % RING
        WO_W = -(-D // (16 * WO_PARTS)) * 16
        WO_COLS = [(n, min(WO_W, D - n)) for n in range(0, D, WO_W)][:WO_PARTS]
        for j, (n0, w_) in enumerate(WO_COLS):
            chunk(("wo", j), (0, kmaj(w_o[0])[:, :, n0:n0 + w_]))
        assert len(chunks) % RING == 0 and sum(w_ for _, w_ in WO_COLS) == D
        STATIC = len(chunks)
        moe_base = list(full_at)
        ff_chunks("moe", moe_w_gate[0, 0], moe_w_up[0, 0], moe_w_down[0, 0])
        FULL_PER = [full_at[s] - moe_base[s] for s in range(RING)]
        MOE_CHUNKS = [l for l, _ in chunks[STATIC:]]
        del chunks[STATIC:]

        def part(label, k, n, at=0):
            return ring[:, where[label][0], at:at + k * n].rearrange("p (k n) -> p k n", k=k)

        fills, place, turn = [0] * BANKS, {}, [0]

        def filled(label):
            b, n = place[label]
            return bank_full[b], n

        def drained(label):
            b, n = place[label]
            return bank_free[b], n

        MOE_FILLS = ([(s, f) for f in range(FT) for s in ("g", "u")] + [("T", i) for i in range(6)]
                     + [("dn", k) for k in range(KT // 2)] + [("sc", i) for i in range(6)] + [("pgT", i) for i in range(NT)]
                     + [("ga", k) for k in range(KT)] + [("dn", k) for k in range(KT // 2, KT)])
        HALF_FILLS = [("g", f0) for f0, _ in GU] + [("dn", 2 * dp) for dp in range(4)]
        HALF_PER = len(HALF_FILLS)
        MOE_PER = [len(MOE_FILLS[b::BANKS]) for b in range(BANKS)]

        def moe_filled(label, e):
            b, n = place[("moe",) + label]
            return bank_full[b], e * MOE_PER[b] + n

        def moe_drained(label, e):
            b, n = place[("moe",) + label]
            return bank_free[b], e * MOE_PER[b] + n

        TILES = [("k", 3), ("k", 0), ("k", 1), ("k", 2), ("q", 0), ("q", 1), ("q", 2)]
        HEAD_TILES = [(h, t) for h in range(MH) for t in range(NT)]
        AHEAD = 3
        TURNS = [(t, g) for t in range(NT) for g in range(GROUPS)]
        w_release, sq_at, used_before_moe, added = {}, {}, [], {}
        ROOTS = ([("n", 0), "v", ("y", 0), ("y", 1), ("y", 2), ("n", 1), ("n", 2), "qa", "ckv"]
                 + [("kq", i) for i in range(7)] + [("n", 3)])

        def root_at(label):
            n = ROOTS.index(label)
            return n + 1, stat[:, 8 * n:8 * n + 8]

        const_dram = nc.inline_tensor(consts_np, name="tables").ap()
        iota_dram = nc.inline_tensor(np.tile(np.arange(TOK, dtype=np.float32), (P, 1)), name="slot_numbers").ap()
        block = ctx.enter_context(nc.Block())

        @block.tensor
        def _(pe):
            mm, tp = nc.tensor.matmul, nc.tensor.transpose

            def fill(label):
                b = turn[0] % BANKS
                turn[0] += 1
                fills[b] += 1
                place[label] = (b, fills[b])
                if fills[b] > 1:
                    pe.wait_ge(bank_free[b], fills[b] - 1)
                return PSUM[b], bank_full[b]

            def landed(label):
                pe.wait_ge(ring_full[where[label][0]], where[label][1])

            used = [0]

            def used_amid(label, last):
                used[0] += 1
                last.then_inc(chunk_used, 1)
                released[label] = (chunk_used, used[0])

            def blocks(label, sources):
                bank, full = fill(label)
                for k, src in enumerate(sources):
                    last = tp(bank[:, k * P:(k + 1) * P], src, ident)
                last.then_inc(full, 1)

            pe.wait_ge(const_loaded, 16)
            pe.wait_ge(banks_zero, 1)
            pe.wait_ge(prow_loaded, 16 * 8)
            bank, full = fill("col")
            tp(bank[:, 0:112], praw[0:112, 0, :], ident[0:112, 0:112])
            tp(bank[:, 112:223], praw[0:111, 1, :], ident[0:111, 0:111]).then_inc(full, 1)

            def to_feature_major(n):
                for t in range(NT):
                    pe.wait_ge(xn_ready, NT * n + t + 1)
                    for half in range(2):
                        blocks(("nt", n, t, half), [XN[:, t, (4 * half + k) * P:(4 * half + k + 1) * P] for k in range(4)])

            def ht_ready(n):
                for t in range(NT):
                    pe.wait_ge(*drained(("nt", n, t, 0)))
                    pe.wait_ge(*drained(("nt", n, t, 1)))

            def mod_rows(layer, j):
                label = ("mod", layer, j)
                landed(label)
                w = part(label, KT, 512)
                bank, full = fill(("mr", layer, j))
                for k in range(KT):
                    q = 32 * (k % 4)
                    last = mm(bank[q:q + 2, :], sv[:, :, k], w[:, k, :], start=(k < 4), stop=(k >= 4))
                last.then_inc(full, 1)
                released[label] = filled(("mr", layer, j))

            def mod_columns(layer, j):
                pe.wait_ge(*drained(("mr", layer, j)))
                bank, full = fill(("mc", layer, j))
                for m in range(4):
                    last = mm(bank[:, 2 * m:2 * m + 2], mrow[:, j % 2, m * P:(m + 1) * P], pick, start=True, stop=True)
                last.then_inc(full, 1)

            def gate_rows(layer, which, n):
                pe.wait_ge(mod_ready, layer + 2)
                for s in range(2):
                    for half in range(2):
                        bank, full = fill(("gb", n, s, half))
                        for k in range(4):
                            m = which * KT + 4 * half + k
                            last = mm(bank[:, k * P:(k + 1) * P], modT[:, layer, m, s:s + 1].to_broadcast([P, P]), ident, start=True, stop=True)
                        last.then_inc(full, 1)

            def token_major(name, label, lhs, kt, width):
                landed(label)
                w = part(label, kt, width)
                for t in range(NT):
                    bank, full = fill((name, t))
                    for k in range(kt):
                        last = mm(bank[:, 0:width], lhs[:, k, t * P:(t + 1) * P], w[:, k, :], start=(k == 0), stop=(k == kt - 1))
                    last.then_inc(full, 1)
                released[label] = filled((name, NT - 1))

            pe.wait_ge(sv_ready, 1)
            mod_rows(0, 0)
            for j in range(4):
                if j + 1 < 4:
                    mod_rows(0, j + 1)
                mod_columns(0, j)
            to_feature_major(0)
            ht_ready(0)

            for j in range(4):
                label = ("xbc", j)
                landed(label)
                w = part(label, KT, 512)
                for m in range(4):
                    bank, full = fill(("xbc", 4 * j + m, "p"))
                    for k in range(KT):
                        last = mm(bank[:, 0:TOK], w[:, k, m * P:(m + 1) * P], HT[:, k, :], start=(k == 0), stop=(k == KT - 1))
                    last.then_inc(full, 1)
                released[label] = filled(("xbc", 4 * j + 3, "p"))
                mod_rows(0, 4 + j)
                if j > 0:
                    mod_columns(0, 3 + j)
                else:
                    pe.wait_ge(wsp_loaded, 16)
                    blocks("wsp", [praw[:, 2 + g, :] for g in range(SGRP)])
            pe.wait_ge(small_loaded, 16 * 9)
            bank, full = fill("dt")
            for t in range(NT):
                for k in range(KT):
                    last = mm(bank[:, 32 * t:32 * t + 32], HT[:, k, t * P:(t + 1) * P], wdt[:, k, :], start=(k == 0), stop=(k == KT - 1))
            last.then_inc(full, 1)
            for name in ("v", "u"):
                for j in range(2):
                    token_major((name, j, "p"), (name, j), HT, KT, 512)
                    mod_rows(0, MOD_WITH[name] + j)
                    mod_columns(0, MOD_WITH[name] + j - 1)
            mod_columns(0, 11)

            pe.wait_ge(*drained("wsp"))
            for t in range(NT):
                pe.wait_ge(vn_ready, t + 1)
                for half in range(2):
                    bank, full = fill(("sg", t, half))
                    for g in range(2):
                        gg = 2 * half + g
                        last = mm(bank[:, g * SGD:(g + 1) * SGD], wspT[:, gg, :], V[:, t, gg * SGD:(gg + 1) * SGD], start=True, stop=True)
                    last.then_inc(full, 1)
            pe.wait_ge(cv_ready, 12)
            for t in range(NT):
                for q in range(3):
                    blocks(("xs", t, q), [CV[:, 4 * q + k, TOK0[t]:TOK0[t] + P] for k in range(4)])
            pe.wait_ge(dta_ready, 1)
            bank, full = fill("cs")
            for t in range(NT):
                for d in range(2):
                    o = 32 * t + 16 * d
                    mm(bank[:, o:o + 16], tri[d], dtA[:, o:o + 16], start=True, stop=True)
            mm(bank[:, 96:192], ones, dtA, start=True, stop=True).then_inc(full, 1)
            pe.wait_ge(cv_ready, CCT)
            for t in range(NT):
                bank, full = fill(("cb", t))
                for g in range(GROUPS):
                    last = mm(bank[:, g * P:(g + 1) * P], CV[:, 8 + g, TOK0[t]:TOK0[t] + P], CV[:, 12 + g, TOK0[t]:TOK0[t] + P], start=True, stop=True)
                last.then_inc(full, 1)
            pe.wait_ge(st_loaded, 16)
            for d in range(2):
                for half in range(2):
                    blocks(("st", d, half), [st_raw[:, d, 4 * half + k, :] for k in range(4)])
            for j in range(2):
                token_major(("z", j, "p"), ("z", j), HT, KT, 512)

            for t in range(NT):
                pe.wait_ge(*drained(("xs", t, 2)))
            for d in range(2):
                pe.wait_ge(xde_ready, d + 1)
                for half in range(2):
                    bank, full = fill(("cst", d, half))
                    for k in range(4):
                        i = 4 * half + k
                        last = mm(bank[:, k * P:(k + 1) * P], W[:, d, i * P:(i + 1) * P], BT[:, 0, (i // 2) * P:(i // 2 + 1) * P], start=True, stop=True)
                    last.then_inc(full, 1)

            def state_output(t, d):
                for half in range(2):
                    bank, full = fill(("off", t, d, half))
                    for g in range(2):
                        gg = 2 * half + g
                        last = mm(bank[:, g * 256:(g + 1) * 256], CV[:, 12 + gg, TOK0[t]:TOK0[t] + P], stT[:, d, gg * 256:(gg + 1) * 256], start=True, stop=True)
                    last.then_inc(full, 1)

            for d in range(2):
                pe.wait_ge(*drained(("st", d, 0)))
                pe.wait_ge(*drained(("st", d, 1)))
            state_output(1, 0)
            state_output(2, 1)
            for d in range(2):
                pe.wait_ge(xde_ready, 3 + d)
                for half in range(2):
                    bank, full = fill(("own", d, half))
                    for g in range(2):
                        gg = 2 * half + g
                        last = mm(bank[:, g * 256:(g + 1) * 256], BT[:, 1 + d, gg * P:(gg + 1) * P], W[:, d, gg * 256:(gg + 1) * 256], start=True, stop=True)
                    last.then_inc(full, 1)
            for d in range(2):
                pe.wait_ge(st_upd, d + 1)
                state_output(2 - d, d)

            def decay_rows(i):
                t, g = TURNS[i]
                for d in range(2):
                    bank, full = fill(("cr", i, d))
                    for h in range(HPG):
                        col = 32 * t + 16 * d + HPG * g + h
                        last = mm(bank[:, h * P:(h + 1) * P], dtA[:, col:col + 1].to_broadcast([P, P]), tri[d], start=True, stop=True)
                    last.then_inc(full, 1)

            pe.wait_ge(xdt_ready, 6)
            decay_rows(0)
            for i, (t, g) in enumerate(TURNS):
                if i + 1 < len(TURNS):
                    decay_rows(i + 1)
                if g % 2 == 0:
                    bank, full = fill(("y", t, g // 2))
                pe.wait_ge(wm_ready, i + 1)
                for h in range(HPG):
                    hh = HPG * g + h
                    for d in range(2):
                        last = mm(bank[:, (hh % 8) * HD:(hh % 8 + 1) * HD], W[:, i % 2, (4 * d + h) * P:(4 * d + h + 1) * P],
                                  xdt[:, t, d, hh * HD:(hh + 1) * HD], start=(d == 0), stop=(d == 1))
                if g % 2 == 0:
                    last.then_inc(w_used, 1)
                    w_release[i] = (w_used, i // 2 + 1)
                else:
                    last.then_inc(full, 1)
                    w_release[i] = filled(("y", t, g // 2))

            gate_rows(0, 2, 0)
            for t in range(NT):
                for half in range(2):
                    blocks(("yu", t, half), [U[:, t, (4 * half + k) * P:(4 * half + k + 1) * P] for k in range(4)])
            for t in range(NT):
                pe.wait_ge(yn_ready, t + 1)
                for half in range(2):
                    blocks(("yy", t, half), [XS[:, t, (4 * half + k) * P:(4 * half + k + 1) * P] for k in range(4)])
            for t in range(NT):
                for half in range(2):
                    pe.wait_ge(*drained(("yu", t, half)))
                    pe.wait_ge(*drained(("yy", t, half)))
            for j in range(4):
                token_major(("wout", j, "p"), ("wout", j), YT, 16, 256)

            gate_rows(0, 5, 1)
            to_feature_major(1)
            ht_ready(1)
            for j, (f0, n) in enumerate(GU):
                label = ("ffn", "gu", j)
                landed(label)
                for m in range(n):
                    for name, at in (("g", 0), ("u", 2048)):
                        w = part(label, KT, n * P, at)
                        bank, full = fill((name, f0 + m))
                        for k in range(KT):
                            last = mm(bank[:, 0:TOK], w[:, k, m * P:(m + 1) * P], HT[:, k, :], start=(k == 0), stop=(k == KT - 1))
                        last.then_inc(full, 1)
                released[label] = filled(("u", f0 + n - 1))
                mod_rows(1, j)
                if j > 0:
                    mod_columns(1, j - 1)
            mod_columns(1, 11)
            pe.wait_ge(*drained(("u", FT - 1)))
            pe.wait_ge(*drained(("u", FT - 2)))
            for dp in range(4):
                banks = [fill(("down", dp, t)) for t in range(NT)]
                for fh in range(2):
                    label = ("ffn", "dn", dp, fh)
                    landed(label)
                    w = part(label, FH, 256)
                    for t in range(NT):
                        for f in range(FH):
                            last = mm(banks[t][0][:, 0:256], aT[:, FH * fh + f, t * P:(t + 1) * P], w[:, f, :],
                                      start=(fh == 0 and f == 0), stop=(fh == 1 and f == FH - 1))
                        if fh == 1:
                            last.then_inc(banks[t][1], 1)
                    if fh == 0:
                        used_amid(label, last)
                    else:
                        released[label] = filled(("down", dp, NT - 1))

            gate_rows(1, 2, 2)
            to_feature_major(2)
            ht_ready(2)
            token_major("dq_p", "dq", HT, KT, QR)
            token_major("dkv_p", "dkv", HT, KT, KVR + ROPE)
            for t in (3, 0, 1, 2):
                if t == 3:
                    pe.wait_ge(cache_loaded, 32)
                else:
                    pe.wait_ge(ckv_ready, t + 1)
                blocks(("ckvT", t), [ckv[:, t, k * P:(k + 1) * P] for k in range(2)])
            for t in range(NT):
                pe.wait_ge(qa_ready, t + 1)
                blocks(("qaT", t), [qa[:, t, k * P:(k + 1) * P] for k in range(3)])

            def expand(i):
                kind, t = TILES[i]
                if kind == "k":
                    if i == 0:
                        landed("ukv")
                    pe.wait_ge(*drained(("ckvT", t)))
                    w = part("ukv", 2, 2048)
                    for j in range(4):
                        bank, full = fill(("kv", t, j))
                        for k in range(2):
                            last = mm(bank[:, :], ckvT[:, k, t * P:(t + 1) * P], w[:, k, 512 * j:512 * j + 512], start=(k == 0), stop=(k == 1))
                        last.then_inc(full, 1)
                    released["ukv"] = filled(("kv", t, 3))
                else:
                    pe.wait_ge(*drained(("qaT", t)))
                    for j in range(4):
                        if t == 0 and j % 2 == 0:
                            landed(("uq", j // 2))
                        w = part(("uq", j // 2), 3, 768)
                        bank, full = fill(("q", t, j))
                        for k in range(3):
                            last = mm(bank[:, 0:384], qaT[:, k, t * P:(t + 1) * P], w[:, k, 384 * (j % 2):384 * (j % 2) + 384], start=(k == 0), stop=(k == 2))
                        last.then_inc(full, 1)
                        released[("uq", j // 2)] = filled(("q", t, j))

            expand(0)
            for i in range(len(TILES)):
                if i + 1 < len(TILES):
                    expand(i + 1)
                pe.wait_ge(kq_ready, i + 1)
                for q in range(2):
                    blocks(("hT", i, q), [KQN[:, i % 2, 4 * q + k, :] for k in range(4)])
                blocks(("hT", i, 2), [kq_v[:, i % 2, D + k * P:D + (k + 1) * P] for k in range(4)])

            for i in range(len(TILES)):
                for q in range(3):
                    pe.wait_ge(*drained(("hT", i, q)))

            def scores(n):
                h, t = HEAD_TILES[n]
                bank, full = fill(("s", n))
                r = 64 * (h % 2)
                k0, kn = (0, P) if t == 0 else (P, 3 * P)
                mm(bank[:, 0:kn], qTn[:, h, t * P:(t + 1) * P], kTn[:, h, k0:k0 + kn], start=True, stop=False)
                mm(bank[:, 0:kn], qTr[r:r + 64, h // 2, t * P:(t + 1) * P], kTr[r:r + 64, h // 2, k0:k0 + kn],
                   start=False, stop=True).then_inc(full, 1)

            def values(h):
                for t in range(NT):
                    pe.wait_ge(*drained(("pT", NT * h + t)))
                bank, full = fill(("o", h))
                mm(bank[:, 0:P], VV[:, 0, h * VH:(h + 1) * VH], PT[:, h % 2, 0:P], start=True, stop=True)
                for k in range(3):
                    last = mm(bank[:, P:3 * P], VV[:, 1 + k, h * VH:(h + 1) * VH], PT[:, h % 2, P + 256 * k:P + 256 * k + 256],
                              start=(k == 0), stop=(k == 2))
                last.then_inc(full, 1)

            for n in range(AHEAD):
                scores(n)
            for n, (h, t) in enumerate(HEAD_TILES):
                if n + AHEAD < len(HEAD_TILES):
                    scores(n + AHEAD)
                pe.wait_ge(pr_ready, n + 1)
                blocks(("pT", n), [PR[:, n % 4, k * P:(k + 1) * P] for k in range(1 if t == 0 else 3)])
                if t == 1 and h > 0:
                    values(h - 1)
            values(MH - 1)
            for h in range(MH):
                pe.wait_ge(*drained(("o", h)))
            for j, (_, w_) in enumerate(WO_COLS):
                token_major(("wo", j, "p"), ("wo", j), OT, KT, w_)

            to_feature_major(3)
            ht_ready(3)
            bank, full = fill("lg")
            for t in range(NT):
                for k in range(KT):
                    last = mm(bank[:, 8 * t:8 * t + 8], HT[:, k, t * P:(t + 1) * P], wrt[:, k, :], start=(k == 0), stop=(k == KT - 1))
            last.then_inc(full, 1)
            for t in range(NT):
                for half in range(2):
                    blocks(("h2", t, half), [HT[:, 4 * half + k, t * P:(t + 1) * P] for k in range(4)])
            pe.wait_ge(sel_ready, 1)
            bank, full = fill("rank")
            for t in range(NT):
                for s in range(t + 1):
                    mm(bank[:, 8 * t:8 * t + 8], before if s == t else ones, sel[:, s, :], start=(s == 0), stop=(s == t))
            for s in range(NT):
                last = mm(bank[:, 24:32], ones, sel[:, s, :], start=(s == 0), stop=(s == NT - 1))
            last.then_inc(full, 1)
            for t in range(NT):
                pe.wait_ge(*drained(("h2", t, 0)))
                pe.wait_ge(*drained(("h2", t, 1)))
            pe.wait_ge(ps_ready, 1)
            for k in range(KT):
                bank, full = fill(("ga0", k))
                for t in range(NT):
                    last = mm(bank[:, 0:TOK], H2[:, t, k * P:(k + 1) * P], PS[:, t, :], start=(t == 0), stop=(t == NT - 1))
                last.then_inc(full, 1)

            for i, label in enumerate(MOE_FILLS):
                place[("moe",) + label] = (i % BANKS, fills[i % BANKS] + i // BANKS + 1)

            def moe_bank(label, e):
                b, n = place[("moe",) + label]
                pe.wait_ge(bank_free[b], e * MOE_PER[b] + (n - 1))
                return PSUM[b], bank_full[b]

            def moe_landed(label, e):
                s, n = where[label]
                pe.wait_ge(ring_full[s], e * FULL_PER[s] + n)

            def turn_outputs(e, slot_tiles):
                for i in range(6):
                    bank, full = moe_bank(("T", i), e)
                    if i // 2 >= slot_tiles:
                        pe.sem_inc(full, 1)
                        continue
                    for k in range(4):
                        last = tp(bank[:, k * P:(k + 1) * P], yT[:, 4 * (i % 2) + k, (i // 2) * P:(i // 2 + 1) * P], ident)
                    last.then_inc(full, 1)

            def scatter(e, slot_tiles):
                for i in range(6):
                    t, half = i // 2, i % 2
                    bank, full = moe_bank(("sc", i), e)
                    for s in range(slot_tiles):
                        last = mm(bank[:, :], PGT[:, s, t * P:(t + 1) * P], yt[:, s, 512 * half:512 * half + 512],
                                  start=(s == 0), stop=(s == slot_tiles - 1))
                    last.then_inc(full, 1)

            def turn_gates(e, slot_tiles):
                for i in range(NT):
                    bank, full = moe_bank(("pgT", i), e)
                    if i >= slot_tiles:
                        pe.sem_inc(full, 1)
                        continue
                    for t in range(NT):
                        last = tp(bank[:, t * P:(t + 1) * P], PG[:, t, i * P:(i + 1) * P], ident)
                    last.then_inc(full, 1)

            def hidden(e, N):
                for j, (f0, n) in enumerate(GU):
                    label = ("moe", "gu", j)
                    moe_landed(label, e)
                    for m in range(n):
                        for name, at in (("g", 0), ("u", 2048)):
                            w = part(label, KT, n * P, at)
                            bank, full = moe_bank((name, f0 + m), e)
                            for k in range(KT):
                                last = mm(bank[:, 0:N], w[:, k, m * P:(m + 1) * P], xeT[:, k, 0:N], start=(k == 0), stop=(k == KT - 1))
                            last.then_inc(full, 1)

            def gather(e, N):
                for k in range(KT):
                    bank, full = moe_bank(("ga", k), e)
                    for t in range(NT):
                        last = mm(bank[:, 0:N], H2[:, t, k * P:(k + 1) * P], PS[:, t, 0:N], start=(t == 0), stop=(t == NT - 1))
                    last.then_inc(full, 1)

            def fold_halves(e, r, targets):
                pe.wait_ge(halves_copied, e * HALF_PER + r + 1)
                for label, at in targets:
                    bank, full = moe_bank(label, e)
                    mm(bank[:, 0:P], halves[:, r % 2, at:at + P], fold, start=True, stop=True).then_inc(full, 1)

            def narrow_hidden(e):
                def products(j):
                    f0, n = GU[j]
                    label = ("moe", "gu", j)
                    moe_landed(label, e)
                    bank, _ = moe_bank(HALF_FILLS[j], e)
                    for to, at in ((0, 0), (256, 2048)):
                        w = part(label, KT, n * P, at)
                        for k in range(KT):
                            q = NARROW * (k % 2)
                            last = mm(bank[q:q + NARROW, to:to + n * P], xeT[:, k, 0:NARROW], w[:, k, :], start=(k < 2), stop=(k >= KT - 2))
                    last.then_inc(halves_full, 1)

                products(0)
                for j, (f0, n) in enumerate(GU):
                    if j + 1 < len(GU):
                        products(j + 1)
                    fold_halves(e, j, [((name, f0 + m), to + m * P) for m in range(n) for name, to in (("g", 0), ("u", 256))])

            def narrow_output(e, dps):
                for dp in dps:
                    bank, _ = moe_bank(("dn", 2 * dp), e)
                    for fh in range(2):
                        label = ("moe", "dn", dp, fh)
                        moe_landed(label, e)
                        w = part(label, FH, 256)
                        for f in range(FH * fh, FH * fh + FH):
                            q = NARROW * (f % 2)
                            last = mm(bank[q:q + NARROW, 0:256], aT[:, f, 0:NARROW], w[:, f - FH * fh, :], start=(f < 2), stop=(f >= FT - 2))
                        last.then_inc(halves_full if fh == 1 else chunk_used, 1)
                for dp in dps:
                    fold_halves(e, len(GU) + dp, [(("dn", 2 * dp + m), m * P) for m in range(2)])

            def output(e, N, dps):
                for dp in dps:
                    banks = [moe_bank(("dn", 2 * dp + m), e) for m in range(2)]
                    for fh in range(2):
                        label = ("moe", "dn", dp, fh)
                        moe_landed(label, e)
                        w = part(label, FH, 256)
                        for m in range(2):
                            for f in range(FH):
                                last = mm(banks[m][0][:, 0:N], w[:, f, m * P:(m + 1) * P], aT[:, FH * fh + f, 0:N],
                                          start=(fh == 0 and f == 0), stop=(fh == 1 and f == FH - 1))
                            if fh == 1:
                                last.then_inc(banks[m][1], 1)
                        if fh == 0:
                            last.then_inc(chunk_used, 1)

            used_before_moe.append(used[0])
            pe.wait_ge(route_ready, 1)
            pe.wait_ge(moe_zero, 3)
            for k in range(KT):
                pe.wait_ge(*drained(("ga0", k)))
            with pe.Fori(0, NE) as e:
                this = pe.value_load(vtab[0:1, 0, bass.ds(e + 1, 1)], min_val=0, max_val=len(WIDTHS) - 1)
                nxt = pe.value_load(vtab[0:1, 0, bass.ds(e + 2, 1)], min_val=0, max_val=len(WIDTHS) - 1)
                prev_tiles = pe.value_load(vtab[0:1, 1, bass.ds(e, 1)], min_val=1, max_val=NT)
                for k in range(KT):
                    pe.wait_ge(*moe_drained(("ga", k), e - 1))
                for v, N in enumerate(WIDTHS):
                    with pe.If(this == v):
                        if N == NARROW:
                            narrow_hidden(e)
                        else:
                            hidden(e, N)
                            pe.sem_inc(halves_full, HALF_PER)
                for k in range(KT):
                    pe.wait_ge(*moe_drained(("dn", k), e - 1))
                for n in range(1, NT + 1):
                    with pe.If(prev_tiles == n):
                        turn_outputs(e, n)
                pe.wait_ge(*moe_drained(("u", FT - 2), e))
                pe.wait_ge(*moe_drained(("u", FT - 1), e))
                for v, N in enumerate(WIDTHS):
                    with pe.If(this == v):
                        if N == NARROW:
                            narrow_output(e, (0, 1))
                        else:
                            output(e, N, (0, 1))
                for i in range(6):
                    pe.wait_ge(*moe_drained(("T", i), e))
                for i in range(NT):
                    pe.wait_ge(*moe_drained(("pgT", i), e - 1))
                for n in range(1, NT + 1):
                    with pe.If(prev_tiles == n):
                        scatter(e, n)
                pe.wait_ge(pg_ready, e + 1)
                for v, N in enumerate(WIDTHS):
                    with pe.If(this == v):
                        turn_gates(e, -(-N // P))
                pe.wait_ge(ps_ready, e + 2)
                for v, N in enumerate(WIDTHS):
                    with pe.If(nxt == v):
                        gather(e, max(N, P))
                for v, N in enumerate(WIDTHS):
                    with pe.If(this == v):
                        if N == NARROW:
                            narrow_output(e, (2, 3))
                        else:
                            output(e, N, (2, 3))
            for b in range(BANKS):
                fills[b] += NE * MOE_PER[b]
            for k in range(KT):
                pe.wait_ge(*moe_drained(("dn", k), NE - 1))
            for i in range(6):
                blocks(("lastT", i), [yT[:, 4 * (i % 2) + k, (i // 2) * P:(i // 2 + 1) * P] for k in range(4)])
            gate_rows(1, 5, 3)
            for i in range(6):
                pe.wait_ge(*drained(("lastT", i)))
            for i in range(NT):
                pe.wait_ge(*moe_drained(("pgT", i), NE - 1))
            last_fills = [fill(("last", i)) for i in range(6)]
            last_tiles = pe.value_load(vtab[0:1, 1, NE:NE + 1], min_val=1, max_val=NT)
            for n in range(1, NT + 1):
                with pe.If(last_tiles == n):
                    for i, (bank, full) in enumerate(last_fills):
                        t, half = i // 2, i % 2
                        for s in range(n):
                            last = mm(bank[:, :], PGT[:, s, t * P:(t + 1) * P], yt[:, s, 512 * half:512 * half + 512], start=(s == 0), stop=(s == n - 1))
                        last.then_inc(full, 1)

        @block.scalar
        def _(act):
            act_fn = nc.scalar.activation
            squares = [0]

            def copy(out, in_):
                return act_fn(out, in_, ACT.Copy)

            def square_sum(label, col, src, junk_):
                if label[0] != "n":
                    act.wait_ge(sq_done, squares[0])
                squares[0] += 1
                sq_at[label] = squares[0]
                act_fn(junk_, src, ACT.Square, accum_out=root_at(label)[1][:, col:col + 1]).then_inc(sq_done, 1)

            def root(label, n):
                i, cols = root_at(label)
                act.wait_ge(ms_ready, i)
                act_fn(cols[:, 0:n], cols[:, 0:n], ACT.Sqrt).then_inc(rt_ready, 1)

            def evacuate(label, pairs):
                act.wait_ge(*filled(label))
                for out, src in pairs:
                    last = copy(out, src)
                last.then_inc(drained(label)[0], 1)

            def bank_of(label):
                return PSUM[place[label][0]]

            def mod_row(layer, j):
                if j >= 2:
                    act.wait_ge(*filled(("mc", layer, j - 2)))
                evacuate(("mr", layer, j), [(mrow[:, j % 2, :], bank_of(("mr", layer, j))[:, :])])

            def norm_squares(n):
                for t in range(NT):
                    if n > 0:
                        act.wait_ge(x_updated, NT * (n - 1) + t + 1)
                    square_sum(("n", n), t, X[:, t, :], XN[:, t, :])

            def modulated(n, layer, i):
                for t in range(NT):
                    s = 0 if t == 0 else 1
                    label = ("nt", n, t, 0)
                    act.wait_ge(*filled(label))
                    for k in range(4):
                        last = act_fn(HT[:, k, t * P:(t + 1) * P], bank_of(label)[:, k * P:(k + 1) * P], ACT.Identity,
                                      bias=modT[:, layer, i * KT + k, s:s + 1], scale=modT[:, layer, (i + 1) * KT + k, s:s + 1])
                    last.then_inc(drained(label)[0], 1)

            def gates(n):
                for s in range(2):
                    for half in range(2):
                        evacuate(("gb", n, s, half), [(GB[:, s, 512 * half:512 * half + 512], bank_of(("gb", n, s, half))[:, :])])

            act.wait_ge(*drained("col"))
            act_fn(sv[:, :, :].rearrange("p s k -> p (s k)"), colT[:, 0, 0:16], ACT.Silu).then_inc(sv_ready, 1)
            for out, src in ((dtb_r, dt_bias.rearrange("a d h -> a (d h)")), (alog_r, a_log.rearrange("a d h -> a (d h)")),
                             (dsk_r, d_skip), (qn_r, q_norm), (kn_r, k_norm), (kvn_r, kv_a_norm), (sgn_r, sgu_norm)):
                act.dma_start(out, src.to_broadcast([P, src.shape[1]])).then_inc(small_loaded, 16)
            act.dma_start(wdt[:, :, :], win[:, :, 3072:3104]).then_inc(small_loaded, 16)
            act.dma_start(wrt[:, :, :], kmaj(router[0])).then_inc(small_loaded, 16)

            for j in range(2):
                mod_row(0, j)
            act.wait_ge(x_loaded, 32)
            norm_squares(0)
            root(("n", 0), NT)
            for j in range(2, 4):
                mod_row(0, j)
            act.wait_ge(mod_ready, 1)
            modulated(0, 0, 0)

            def conv_silu(ct):
                act.wait_ge(conv_done, ct + 1)
                act_fn(CV[:, ct, :], CV[:, ct, :], ACT.Silu).then_inc(cv_ready, 1)

            act.wait_ge(raw_zero, 1)
            for ct in range(CCT):
                if ct >= 4:
                    act.wait_ge(conv_done, ct - 3)
                b = bank_of(("xbc", ct, "p"))
                evacuate(("xbc", ct, "p"), [(raw[:, ct % 4, PAD:PAD + P], b[:, 0:P]),
                                            (raw[:, ct % 4, 2 * PAD + P:2 * PAD + P + LAT], b[:, P:TOK])])
                if ct % 4 == 3:
                    mod_row(0, 4 + ct // 4)
                if ct == 3:
                    evacuate("wsp", [(wspT[:, :, :].rearrange("p g t -> p (g t)"), bank_of("wsp")[:, :])])
                if ct >= 2:
                    conv_silu(ct - 2)
            conv_silu(14)
            conv_silu(15)
            act.wait_ge(dt_arg, 1)
            act_fn(dtu, dtw, ACT.Exp).then_inc(dt_exp, 1)
            act.wait_ge(small_loaded, 16 * 9)
            act_fn(aexp, alog_r, ACT.Exp).then_inc(dt_exp, 1)
            act.wait_ge(dt_w, 1)
            act_fn(dtv, dtw, ACT.Ln).then_inc(dt_ln, 1)
            for j in range(2):
                for t in range(NT):
                    evacuate((("v", j, "p"), t), [(V[:, t, 512 * j:512 * j + 512], bank_of((("v", j, "p"), t))[:, :])])
                mod_row(0, MOD_WITH["v"] + j)
            for t in range(NT):
                for j in range(2):
                    act.wait_ge(*drained((("v", j, "p"), t)))
                square_sum("v", t, V[:, t, :], Z[:, t, :])
            root("v", NT)
            for j in range(2):
                for t in range(NT):
                    evacuate((("u", j, "p"), t), [(U[:, t, 512 * j:512 * j + 512], bank_of((("u", j, "p"), t))[:, :])])
                mod_row(0, MOD_WITH["u"] + j)
            for t in range(NT):
                evacuate(("xs", t, 0), [(XS[:, t, 0:512], bank_of(("xs", t, 0))[:, :])])
                evacuate(("xs", t, 2), [(BT[:, t, :], bank_of(("xs", t, 2))[:, :])])
            act.wait_ge(cs_ready, 1)
            act_fn(ecs, csn, ACT.Exp, scale=-1.0).then_inc(ex_ready, 1)
            act.wait_ge(end_ready, 1)
            act_fn(den, den, ACT.Exp).then_inc(ex_ready, 1)
            act_fn(etot, tot, ACT.Exp).then_inc(ex_ready, 1)
            for t in range(NT):
                evacuate(("cb", t), [(cb[:, t, :, :].rearrange("p g l -> p (g l)"), bank_of(("cb", t))[:, :])])
            for d in range(2):
                for half in range(2):
                    evacuate(("st", d, half), [(stT[:, d, 512 * half:512 * half + 512], bank_of(("st", d, half))[:, :])])
            for j in range(2):
                for t in range(NT):
                    label = (("z", j, "p"), t)
                    act.wait_ge(*filled(label))
                    act_fn(Z[:, t, 512 * j:512 * j + 512], bank_of(label)[:, :], ACT.Silu).then_inc(drained(label)[0], 1)
            for d in range(2):
                for half in range(2):
                    evacuate(("cst", d, half), [(cst[:, d, 4 * half:4 * half + 4, :].rearrange("p i n -> p (i n)"), bank_of(("cst", d, half))[:, :])])
            for i in range(len(TURNS)):
                act.wait_ge(arg_ready, i + 1)
                act_fn(W[:, i % 2, :], W[:, i % 2, :], ACT.Exp).then_inc(exp_ready, 1)
            gates(0)
            act.wait_ge(state_out, 32)
            for t in range(NT):
                for half in range(2):
                    label = ("yu", t, half)
                    evacuate(label, [(YT[:, 8 + 4 * half:12 + 4 * half, t * P:(t + 1) * P], bank_of(label)[:, :].rearrange("p (k t) -> p k t", k=4))])
            for t in range(NT):
                act.wait_ge(y_ready, t + 1)
                square_sum(("y", t), 0, XS[:, t, :], sgn_r)
                root(("y", t), 1)
            for t in range(NT):
                label = ("yy", t, 0)
                act.wait_ge(*filled(label))
                for k in range(4):
                    last = act_fn(YT[:, k, t * P:(t + 1) * P], bank_of(label)[:, k * P:(k + 1) * P], ACT.Copy, scale=ssdn[:, k:k + 1])
                last.then_inc(drained(label)[0], 1)

            norm_squares(1)
            root(("n", 1), NT)
            gates(1)
            modulated(1, 0, 3)
            for f in range(FT):
                act.wait_ge(*filled(("g", f)))
                if f >= 2:
                    act.wait_ge(*drained(("u", f - 2)))
                act_fn(sg[:, f % 2, :], bank_of(("g", f))[:, 0:TOK], ACT.Silu).then_inc(drained(("g", f))[0], 1)
                if f in GU_LAST:
                    mod_row(1, GU_LAST.index(f))

            norm_squares(2)
            root(("n", 2), NT)
            act.wait_ge(mod_ready, 3)
            gates(2)
            modulated(2, 1, 0)
            for t in range(NT):
                evacuate(("dq_p", t), [(qa[:, t, :], bank_of(("dq_p", t))[:, 0:QR])])
            for t in range(NT):
                act.wait_ge(*drained(("dq_p", t)))
                square_sum("qa", t, qa[:, t, :], junk[:, 0:QR])
            root("qa", NT)
            for t in range(NT):
                evacuate(("dkv_p", t), [(ckv[:, t, :], bank_of(("dkv_p", t))[:, 0:KVR]), (kpe[:, t, :], bank_of(("dkv_p", t))[:, KVR:KVR + ROPE])])
            for t in range(NT):
                act.wait_ge(*drained(("dkv_p", t)))
                square_sum("ckv", t, ckv[:, t, :], junk[:, QR:QR + KVR])
            root("ckv", NT)
            for t in (3, 0, 1, 2):
                evacuate(("ckvT", t), [(ckvT[:, :, t * P:(t + 1) * P], bank_of(("ckvT", t))[:, 0:2 * P].rearrange("p (k t) -> p k t", k=2))])
            for t in range(NT):
                label = ("qaT", t)
                act.wait_ge(*filled(label))
                for k in range(3):
                    last = act_fn(qaT[:, k, t * P:(t + 1) * P], bank_of(label)[:, k * P:(k + 1) * P], ACT.Copy, scale=qanc[:, k:k + 1])
                last.then_inc(drained(label)[0], 1)

            def expanded(i):
                kind, t = TILES[i]
                if i >= 2:
                    act.wait_ge(*filled(("hT", i - 2, 2)))
                for j in range(4):
                    if kind == "k":
                        b = bank_of(("kv", t, j))[:, :].rearrange("p (h n) -> p h n", h=2)
                        evacuate(("kv", t, j), [(KQN[:, i % 2, 2 * j:2 * j + 2, :], b[:, :, 0:NOPE]),
                                                (VV[:, t, 256 * j:256 * j + 256].rearrange("p (h n) -> p h n", h=2), b[:, :, NOPE:])])
                    else:
                        b = bank_of(("q", t, j))[:, 0:384].rearrange("p (h n) -> p h n", h=2)
                        evacuate(("q", t, j), [(KQN[:, i % 2, 2 * j:2 * j + 2, :], b[:, :, 0:NOPE]),
                                               (KQR[:, i % 2, 2 * j:2 * j + 2, :], b[:, :, NOPE:])])
                if kind == "k":
                    act.wait_ge(ckv_ready, 3)
                    if t == 3:
                        act.wait_ge(cache_loaded, 32)
                    copy(KQR[:, i % 2, :, :], kpe[:, t, :].unsqueeze(1).broadcast_to([P, MH, ROPE])).then_inc(kpe_ready, 1)
                    act.wait_ge(kpe_ready, i + 1)
                for j in range(4):
                    act.wait_ge(*drained((kind if kind == "q" else "kv", t, j)))
                if i > 0:
                    act.wait_ge(kq_ready, i)
                squares[0] += 1
                sq_at[("kq", i)] = squares[0]
                act_fn(junk, kq_v[:, i % 2, :], ACT.Square).then_inc(sq_done, 1)
                root(("kq", i), MH)

            def turned(i):
                kind, t = TILES[i]
                n_to, r_to = (kTn, kTr) if kind == "k" else (qTn, qTr)
                evacuate(("hT", i, 0), [(n_to[:, 0:4, t * P:(t + 1) * P], bank_of(("hT", i, 0))[:, :].rearrange("p (k t) -> p k t", k=4))])
                evacuate(("hT", i, 2), [(r_to[:, :, t * P:(t + 1) * P], bank_of(("hT", i, 2))[:, :].rearrange("p (k t) -> p k t", k=4))])

            for i in range(len(TILES)):
                expanded(i)
                if i > 0:
                    turned(i - 1)
            turned(len(TILES) - 1)

            def probs_turned(n):
                h, t = HEAD_TILES[n]
                b = bank_of(("pT", n))
                if t == 0:
                    pair = (PT[:, h % 2, 0:P], b[:, 0:P])
                else:
                    pair = (PT[:, h % 2, P:896].rearrange("p (k q) -> p k q", k=3)[:, :, (t - 1) * P:t * P],
                            b[:, 0:TOK].rearrange("p (k q) -> p k q", k=3))
                evacuate(("pT", n), [pair])

            for n, (h, t) in enumerate(HEAD_TILES):
                kn = P if t == 0 else TOK
                act.wait_ge(mx_ready, n + 1)
                if n >= 4:
                    act.wait_ge(*filled(("pT", n - 4)))
                act_fn(PR[:, n % 4, 0:kn], bank_of(("s", n))[:, 0:kn], ACT.Exp, bias=nmx[:, n:n + 1], scale=QK ** -0.5,
                       accum_out=psum_[:, n:n + 1]).then_inc(drained(("s", n))[0], 1)
                if n >= 2:
                    probs_turned(n - 2)
            probs_turned(len(HEAD_TILES) - 2)
            probs_turned(len(HEAD_TILES) - 1)

            norm_squares(3)
            root(("n", 3), NT)
            modulated(3, 1, 3)
            act.wait_ge(ex8_arg, 1)
            act_fn(gpair[:, 0:3], gpair[:, 0:3], ACT.Exp).then_inc(ex8_ready, 1)
            for t in range(NT):
                evacuate(("h2", t, 0), [(H2[:, t, 0:512], bank_of(("h2", t, 0))[:, :])])
            for k in range(KT):
                evacuate(("ga0", k), [(xeT[:, k, :], bank_of(("ga0", k))[:, 0:TOK])])

            def moe_evacuate(label, e, out, in_):
                act.wait_ge(*moe_filled(label, e))
                copy(out, in_).then_inc(moe_drained(label, e)[0], 1)

            def moe_bank_of(label):
                return PSUM[place[("moe",) + label][0]]

            def gate_silu(e, f):
                act.wait_ge(*moe_filled(("g", f), e))
                if f >= 2:
                    act.wait_ge(*moe_drained(("u", f - 2), e))
                act_fn(sg[:, f % 2, :], moe_bank_of(("g", f))[:, 0:TOK], ACT.Silu).then_inc(moe_drained(("g", f), e)[0], 1)

            def copy_halves(e, r):
                act.wait_ge(halves_full, e * HALF_PER + r + 1)
                if r >= 2:
                    before_ = ("u", GU_LAST[r - 2]) if r - 2 < len(GU) else ("dn", 2 * (r - 2 - len(GU)) + 1)
                    act.wait_ge(*moe_filled(before_, e))
                copy(halves[:, r % 2, :], moe_bank_of(HALF_FILLS[r])[:, :]).then_inc(halves_copied, 1)

            act.wait_ge(route_ready, 1)
            act.wait_ge(moe_zero, 3)
            with act.Fori(0, NE) as e:
                this = act.value_load(vtab[0:1, 0, bass.ds(e + 1, 1)], min_val=0, max_val=len(WIDTHS) - 1)
                with act.If(this == 0):
                    copy_halves(e, 0)
                    for j, (f0, n) in enumerate(GU):
                        if j + 1 < len(GU):
                            copy_halves(e, j + 1)
                        for m in range(n):
                            gate_silu(e, f0 + m)
                with act.If(this > 0):
                    act.sem_inc(halves_copied, HALF_PER)
                    for f in range(FT):
                        gate_silu(e, f)
                for i in (0, 2, 4):
                    moe_evacuate(("T", i), e, yt[:, i // 2, 0:512], moe_bank_of(("T", i))[:, :])
                with act.If(this == 0):
                    for dp in (0, 1):
                        copy_halves(e, len(GU) + dp)
                for k in (1, 3):
                    moe_evacuate(("dn", k), e, yT[:, k, :], moe_bank_of(("dn", k))[:, 0:TOK])
                for i in range(NT):
                    moe_evacuate(("pgT", i), e, PGT[:, i, :], moe_bank_of(("pgT", i))[:, 0:TOK])
                for k in range(KT):
                    moe_evacuate(("ga", k), e, xeT[:, k, :], moe_bank_of(("ga", k))[:, 0:TOK])
                with act.If(this == 0):
                    for dp in (2, 3):
                        copy_halves(e, len(GU) + dp)
                for k in (5, 7):
                    moe_evacuate(("dn", k), e, yT[:, k, :], moe_bank_of(("dn", k))[:, 0:TOK])
            for i in (0, 2, 4):
                evacuate(("lastT", i), [(yt[:, i // 2, 0:512], bank_of(("lastT", i))[:, :])])
            gates(3)

        @block.vector
        def _(dve):
            v = nc.vector
            steps = [0]

            def then(ins):
                steps[0] += 1
                ins.then_inc(dve_step, 1)
                dve.wait_ge(dve_step, steps[0])

            def note(ins):
                steps[0] += 1
                ins.then_inc(dve_step, 1)
                return steps[0]

            def bank_of(label):
                return PSUM[place[label][0]]

            def inverse_root(label, n, width):
                i, cols = root_at(label)
                cols = cols[:, 0:n]
                v.tensor_scalar(cols, cols, 1.0 / width, EPS, ALU.mult, ALU.add).then_inc(ms_ready, 1)
                dve.wait_ge(rt_ready, i)
                then(v.reciprocal(cols, cols))
                return root_at(label)[1]

            def normalise(n):
                dve.wait_ge(sq_done, sq_at[("n", n)])
                r = inverse_root(("n", n), NT, D)
                for t in range(NT):
                    v.tensor_scalar(XN[:, t, :], X[:, t, :], r[:, t:t + 1], None, ALU.mult).then_inc(xn_ready, 1)

            def modulated(n, layer, i):
                for t in range(NT):
                    s = 0 if t == 0 else 1
                    label = ("nt", n, t, 1)
                    dve.wait_ge(*filled(label))
                    for k in range(4, 8):
                        last = v.tensor_scalar(HT[:, k, t * P:(t + 1) * P], bank_of(label)[:, (k - 4) * P:(k - 3) * P],
                                               modT[:, layer, (i + 1) * KT + k, s:s + 1], modT[:, layer, i * KT + k, s:s + 1], ALU.mult, ALU.add)
                    last.then_inc(drained(label)[0], 1)

            def add_bias(layer, j):
                label = ("mc", layer, j)
                dve.wait_ge(*filled(label))
                v.tensor_tensor(modT[:, layer, 4 * j:4 * j + 4, :], bank_of(label)[:, 0:8].rearrange("p (m s) -> p m s", s=2),
                                bmodc[:, layer, 4 * j:4 * j + 4].unsqueeze(2).broadcast_to([P, 4, 2]), ALU.add).then_inc(drained(label)[0], 1)

            def one_plus_scale(layer, js, scales):
                for j in js:
                    dve.wait_ge(*drained(("mc", layer, j)))
                for i in scales:
                    sc = modT[:, layer, i * KT:(i + 1) * KT, :]
                    last = v.tensor_scalar(sc, sc, 1.0, None, ALU.add)
                last.then_inc(mod_ready, 1)
                dve.wait_ge(mod_ready, 1 if js[-1] == 3 else layer + 2)

            def gated_update(name, j, n0, width, final, n):
                if j == 0:
                    added.clear()
                for t in range(NT):
                    s = 0 if t == 0 else 1
                    label = (name, j, t) if name == "down" else ((name, j, "p"), t)
                    if t == 0 and j == 0:
                        for ss in range(2):
                            for half in range(2):
                                dve.wait_ge(*drained(("gb", n, ss, half)))
                    dve.wait_ge(*filled(label))
                    turn_ = NT * j + t
                    if turn_ >= 2:
                        dve.wait_ge(*added[turn_ - 2])
                    o = ftmp[:, turn_ % 2, 0:width]
                    v.tensor_tensor(o, bank_of(label)[:, 0:width], GB[:, s, n0:n0 + width], ALU.mult).then_inc(drained(label)[0], 1)
                    dve.wait_ge(*drained(label))
                    x = X[:, t, n0:n0 + width]
                    last = v.tensor_tensor(x, x, o, ALU.add)
                    if final:
                        last.then_inc(x_updated, 1)
                        added[turn_] = (x_updated, NT * n + t + 1)
                    else:
                        added[turn_] = (dve_step, note(last))

            for b in range(BANKS):
                last = v.memset(PSUM[b][:, :], 0.0)
            last.then_inc(banks_zero, 1)
            v.memset(raw_a, 0.0).then_inc(raw_zero, 1)
            dve.wait_ge(*filled("col"))
            v.tensor_copy(colT[:, 0, :], bank_of("col")[:, 0:112])
            v.tensor_copy(colT[:, 1, 0:111], bank_of("col")[:, 112:223]).then_inc(drained("col")[0], 1)
            dve.wait_ge(*drained("col"))
            for j in range(4):
                add_bias(0, j)
                if j == 0:
                    normalise(0)
            one_plus_scale(0, range(4), (1,))
            modulated(0, 0, 0)
            for ct in range(CCT):
                dve.wait_ge(*drained(("xbc", ct, "p")))
                o = CV[:, ct, :]
                then(v.tensor_scalar(o, raw[:, ct % 4, 0:CVW], convw[:, 0, ct:ct + 1], convb[:, ct:ct + 1], ALU.mult, ALU.add))
                for i in range(1, CW):
                    ins = v.scalar_tensor_tensor(o, raw[:, ct % 4, i:i + CVW], convw[:, i, ct:ct + 1], o, ALU.mult, ALU.add)
                    if i < CW - 1:
                        then(ins)
                    else:
                        ins.then_inc(conv_done, 1)
                if ct in (7, 11, 15):
                    add_bias(0, ct // 4 + 3)
            dve.wait_ge(small_loaded, 16 * 9)
            dve.wait_ge(*filled("dt"))
            v.tensor_tensor(dtx.rearrange("p (t n) -> p t n", t=NT), bank_of("dt")[:, 0:96].rearrange("p (t n) -> p t n", t=NT),
                            dtb_r.unsqueeze(1).broadcast_to([P, NT, 32]), ALU.add).then_inc(drained("dt")[0], 1)
            dve.wait_ge(*drained("dt"))
            then(v.tensor_scalar(dtw, dtx, -1.0, None, ALU.mult))
            v.tensor_tensor(dtw, dtw, dtx, ALU.min).then_inc(dt_arg, 1)
            dve.wait_ge(dt_exp, 1)
            v.tensor_scalar(dtw, dtu, 1.0, None, ALU.add).then_inc(dt_w, 1)
            dve.wait_ge(dt_ln, 1)
            then(v.tensor_scalar(dtw, dtw, -1.0, None, ALU.add))
            then(v.tensor_scalar(dtA, dtw, 0.0, None, ALU.is_equal))
            then(v.tensor_tensor(dtA, dtA, dtu, ALU.mult))
            then(v.tensor_scalar(dtw, dtw, 2.0 ** -24, None, ALU.max))
            then(v.reciprocal(dtw, dtw))
            then(v.tensor_tensor(dtw, dtw, dtu, ALU.mult))
            then(v.tensor_tensor(dtv, dtv, dtw, ALU.mult))
            then(v.tensor_tensor(dtv, dtv, dtA, ALU.add))
            v.scalar_tensor_tensor(dtt, dtx, 0.0, dtv, ALU.max, ALU.add).then_inc(dt_ready, 1)
            dve.wait_ge(dt_ready, 1)
            dve.wait_ge(dt_exp, 2)
            v.scalar_tensor_tensor(dtA.rearrange("p (t n) -> p t n", t=NT), dtt.rearrange("p (t n) -> p t n", t=NT), -1.0,
                                   aexp.unsqueeze(1).broadcast_to([P, NT, 32]), ALU.mult, ALU.mult).then_inc(dta_ready, 1)
            for j in (7, 8):
                add_bias(0, j)
            dve.wait_ge(sq_done, sq_at["v"])
            r = inverse_root("v", NT, D)
            for t in range(NT):
                v.scalar_tensor_tensor(V[:, t, :], V[:, t, :], r[:, t:t + 1], sgn_r, ALU.mult, ALU.mult).then_inc(vn_ready, 1)
            for j in (9, 10, 11):
                add_bias(0, j)
            for t in range(NT):
                for half in range(2):
                    label = ("sg", t, half)
                    dve.wait_ge(*filled(label))
                    dve.wait_ge(*drained((("u", half, "p"), t)))
                    for g in range(2):
                        gg = 2 * half + g
                        uu = U[:, t, gg * SGD:(gg + 1) * SGD]
                        last = v.scalar_tensor_tensor(uu, bank_of(label)[:, g * SGD:(g + 1) * SGD], bspc[:, gg:gg + 1], uu, ALU.add, ALU.mult)
                    last.then_inc(drained(label)[0], 1)
            one_plus_scale(0, range(12), (4,))
            for t in range(NT):
                dve.wait_ge(*filled(("xs", t, 1)))
                v.tensor_copy(XS[:, t, 512:1024], bank_of(("xs", t, 1))[:, :]).then_inc(drained(("xs", t, 1))[0], 1)
            dve.wait_ge(*filled("cs"))
            v.tensor_scalar(csn, bank_of("cs")[:, 0:96], -1.0, None, ALU.mult).then_inc(cs_ready, 1)
            v.tensor_copy(tot, bank_of("cs")[:, 96:192]).then_inc(drained("cs")[0], 1)
            dve.wait_ge(*drained("cs"))
            dve.wait_ge(cs_ready, 1)
            v.tensor_tensor(den, tot, csn, ALU.add).then_inc(end_ready, 1)
            dve.wait_ge(xdt_ready, 6)
            for t in range(NT):
                xs = XS[:, t, :].rearrange("p (h d) -> p h d", h=HEADS)
                then(v.tensor_tensor(xs, xs, dsk_r.unsqueeze(2).broadcast_to([P, HEADS, HD]), ALU.mult))

            def add_state_output(t, d):
                for half in range(2):
                    label = ("off", t, d, half)
                    dve.wait_ge(*filled(label))
                    o = off[:, half, :]
                    e8_ = ecs[:, 32 * t + 16 * d + 8 * half:32 * t + 16 * d + 8 * half + 8]
                    v.tensor_tensor(o.rearrange("p (h d) -> p h d", h=8), bank_of(label)[:, :].rearrange("p (h d) -> p h d", h=8),
                                    e8_.unsqueeze(2).broadcast_to([P, 8, HD]), ALU.mult).then_inc(drained(label)[0], 1)
                    dve.wait_ge(*drained(label))
                    xs = XS[:, t, 512 * half:512 * half + 512]
                    then(v.tensor_tensor(xs, xs, o, ALU.add))

            dve.wait_ge(ex_ready, 3)
            add_state_output(1, 0)
            add_state_output(2, 1)
            for d in range(2):
                dve.wait_ge(*filled(("own", d, 0)))
                dve.wait_ge(*filled(("own", d, 1)))
                s3 = stT[:, d, :].rearrange("p (h d) -> p h d", h=HEADS)
                o = 32 * (1 + d) + 16 * d
                then(v.tensor_tensor(s3, s3, etot[:, o:o + 16].unsqueeze(2).broadcast_to([P, HEADS, HD]), ALU.mult))
                for half in range(2):
                    s2 = stT[:, d, 512 * half:512 * half + 512]
                    v.tensor_tensor(s2, s2, bank_of(("own", d, half))[:, :], ALU.add).then_inc(drained(("own", d, half))[0], 1)
                dve.wait_ge(*drained(("own", d, 0)))
                dve.wait_ge(*drained(("own", d, 1)))
                dve.nop().then_inc(st_upd, 1)
            add_state_output(2, 0)
            add_state_output(1, 1)

            def scan_args(i):
                t, g = TURNS[i]
                if i >= 2:
                    dve.wait_ge(*w_release[i - 2])
                for d in range(2):
                    label = ("cr", i, d)
                    dve.wait_ge(*filled(label))
                    for h in range(HPG):
                        col = 32 * t + 16 * d + HPG * g + h
                        last = v.scalar_tensor_tensor(W[:, i % 2, (4 * d + h) * P:(4 * d + h + 1) * P], bank_of(label)[:, h * P:(h + 1) * P],
                                                      csn[:, col:col + 1], mask[d], ALU.add, ALU.min)
                    last.then_inc(drained(label)[0], 1)
                dve.wait_ge(*drained(("cr", i, 0)))
                dve.wait_ge(*drained(("cr", i, 1)))
                dve.nop().then_inc(arg_ready, 1)

            def add_scan(t, half):
                label = ("y", t, half)
                dve.wait_ge(*filled(label))
                xs = XS[:, t, 512 * half:512 * half + 512]
                v.tensor_tensor(xs, xs, bank_of(label)[:, :], ALU.add).then_inc(drained(label)[0], 1)
                if half == 1:
                    dve.wait_ge(*drained(("y", t, 0)))
                    dve.wait_ge(*drained(label))
                    v.tensor_tensor(XS[:, t, :], XS[:, t, :], Z[:, t, :], ALU.mult).then_inc(y_ready, 1)

            for j in range(2):
                for t in range(NT):
                    dve.wait_ge(*drained((("z", j, "p"), t)))
            scan_args(0)
            for i, (t, g) in enumerate(TURNS):
                if i + 1 < len(TURNS):
                    scan_args(i + 1)
                if g % 2 == 1:
                    add_scan(t, g // 2)
            for t in range(NT):
                dve.wait_ge(sq_done, sq_at[("y", t)])
                r = inverse_root(("y", t), 1, D)
                v.tensor_scalar(XS[:, t, :], XS[:, t, :], r[:, 0:1], None, ALU.mult).then_inc(yn_ready, 1)
            for t in range(NT):
                label = ("yy", t, 1)
                dve.wait_ge(*filled(label))
                for k in range(4, 8):
                    last = v.tensor_scalar(YT[:, k, t * P:(t + 1) * P], bank_of(label)[:, (k - 4) * P:(k - 3) * P], ssdn[:, k:k + 1], None, ALU.mult)
                last.then_inc(drained(label)[0], 1)
            for j in range(4):
                gated_update("wout", j, 256 * j, 256, j == 3, 0)
            dve.wait_ge(x_updated, NT)
            normalise(1)
            modulated(1, 0, 3)

            for f in range(FT):
                dve.wait_ge(*drained(("g", f)))
                dve.wait_ge(*filled(("u", f)))
                v.tensor_tensor(aT[:, f, :], sg[:, f % 2, :], bank_of(("u", f))[:, 0:TOK], ALU.mult).then_inc(drained(("u", f))[0], 1)
                if f in GU_LAST and f > 1:
                    add_bias(1, GU_LAST.index(f) - 1)
            add_bias(1, 11)
            one_plus_scale(1, range(12), (1, 4))
            for dp in range(4):
                gated_update("down", dp, 256 * dp, 256, dp == 3, 1)

            dve.wait_ge(x_updated, 2 * NT)
            normalise(2)
            modulated(2, 1, 0)
            dve.wait_ge(sq_done, sq_at["qa"])
            r = inverse_root("qa", NT, QR)
            for t in range(NT):
                v.tensor_scalar(qa[:, t, :], qa[:, t, :], r[:, t:t + 1], None, ALU.mult).then_inc(qa_ready, 1)
            dve.wait_ge(sq_done, sq_at["ckv"])
            r = inverse_root("ckv", NT, KVR)
            for t in range(NT):
                v.scalar_tensor_tensor(ckv[:, t, :], ckv[:, t, :], r[:, t:t + 1], kvn_r, ALU.mult, ALU.mult).then_inc(ckv_ready, 1)

            def head_norm(i):
                kind, t = TILES[i]
                b = i % 2
                i_root, cols = root_at(("kq", i))
                dve.wait_ge(sq_done, sq_at[("kq", i)])
                then(v.tensor_reduce(cols, junk[:, 0:D].rearrange("p (h n) -> p h n", h=MH), AXX, ALU.add))
                hr = small[:, 256:264]
                then(v.tensor_reduce(hr, junk[:, D:].rearrange("p (h n) -> p h n", h=MH), AXX, ALU.add))
                then(v.tensor_tensor(cols, cols, hr, ALU.add))
                r = inverse_root(("kq", i), MH, QK)
                gain = kn_r if kind == "k" else qn_r
                for h in range(MH):
                    kn_, kr_ = KQN[:, b, h, :], KQR[:, b, h, :]
                    v.scalar_tensor_tensor(kn_, kn_, r[:, h:h + 1], gain[:, 0:NOPE], ALU.mult, ALU.mult)
                    last = v.scalar_tensor_tensor(kr_, kr_, r[:, h:h + 1], gain[:, NOPE:], ALU.mult, ALU.mult)
                if t not in (1, 2):
                    last.then_inc(kq_ready, 1)
                    return
                then(last)
                pe_ = KQR[:, b, :, :].rearrange("p h (a f m) -> p h a f m", a=2, f=2)
                x1, x2 = pe_[:, :, :, 0, :], pe_[:, :, :, 1, :]
                co = cosT[t - 1].unsqueeze(1).broadcast_to([P, MH, 2, 16])
                si = sinT[t - 1].unsqueeze(1).broadcast_to([P, MH, 2, 16])
                v.tensor_tensor(rt[:, 0], x1, co, ALU.mult)
                v.tensor_tensor(rt[:, 1], x2, si, ALU.mult)
                v.tensor_tensor(rt[:, 2], x1, si, ALU.mult)
                then(v.tensor_tensor(rt[:, 3], x2, co, ALU.mult))
                v.tensor_tensor(x1, rt[:, 0], rt[:, 1], ALU.subtract)
                v.tensor_tensor(x2, rt[:, 2], rt[:, 3], ALU.add).then_inc(kq_ready, 1)

            def turned(i):
                kind, t = TILES[i]
                n_to = kTn if kind == "k" else qTn
                label = ("hT", i, 1)
                dve.wait_ge(*filled(label))
                v.tensor_copy(n_to[:, 4:8, t * P:(t + 1) * P], bank_of(label)[:, :].rearrange("p (k t) -> p k t", k=4)).then_inc(drained(label)[0], 1)

            for i in range(len(TILES)):
                head_norm(i)
                if i > 0:
                    turned(i - 1)
            turned(len(TILES) - 1)

            def maximum(n):
                h, t = HEAD_TILES[n]
                kn = P if t == 0 else TOK
                dve.wait_ge(*filled(("s", n)))
                then(v.reduce_max(nmx[:, n:n + 1], bank_of(("s", n))[:, 0:kn], AXX))
                v.tensor_scalar(nmx[:, n:n + 1], nmx[:, n:n + 1], -QK ** -0.5, None, ALU.mult).then_inc(mx_ready, 1)

            def head_out(h):
                dve.wait_ge(*filled(("o", h)))
                v.tensor_copy(OT[:, h, :], bank_of(("o", h))[:, 0:TOK]).then_inc(drained(("o", h))[0], 1)

            maximum(0)
            maximum(1)
            for n, (h, t) in enumerate(HEAD_TILES):
                kn = P if t == 0 else TOK
                if n + 2 < len(HEAD_TILES):
                    maximum(n + 2)
                dve.wait_ge(*drained(("s", n)))
                then(v.reciprocal(psum_[:, n:n + 1], psum_[:, n:n + 1]))
                pr = PR[:, n % 4, 0:kn]
                v.tensor_scalar(pr, pr, psum_[:, n:n + 1], None, ALU.mult).then_inc(pr_ready, 1)
                if t == 2 and h > 0:
                    head_out(h - 1)
            head_out(MH - 1)
            for j, (n0, w_) in enumerate(WO_COLS):
                gated_update("wo", j, n0, w_, j == len(WO_COLS) - 1, 2)

            dve.wait_ge(x_updated, 3 * NT)
            normalise(3)
            modulated(3, 1, 3)
            dve.wait_ge(iota_loaded, 16)
            dve.wait_ge(*filled("lg"))
            v.tensor_copy(lg, bank_of("lg")[:, 0:24].rearrange("p (t e) -> p t e", t=NT)).then_inc(drained("lg")[0], 1)
            dve.wait_ge(*drained("lg"))
            for t in range(NT):
                then(v.max(top[:, t, :], lg[:, t, :]))
                then(v.max_index(idxu[:, t, :], top[:, t, :], lg[:, t, :]))
            then(v.tensor_copy(idxf, idxu[:, :, :]))
            for t in range(NT):
                v.tensor_scalar(oh1[:, t, :], iota[:, 0:8], idxf[:, t, 0:1], None, ALU.is_equal)
                then(v.tensor_scalar(sel[:, t, :], iota[:, 0:8], idxf[:, t, 1:2], None, ALU.is_equal))
            v.tensor_tensor(gpair[:, 0:3], top[:, :, 1], top[:, :, 0], ALU.subtract).then_inc(ex8_arg, 1)
            dve.wait_ge(ex8_ready, 1)
            then(v.tensor_scalar(gpair[:, 3:6], gpair[:, 0:3], 1.0, None, ALU.add))
            then(v.reciprocal(gpair[:, 3:6], gpair[:, 3:6]))
            then(v.tensor_tensor(gpair[:, 6:9], gpair[:, 0:3], gpair[:, 3:6], ALU.mult))
            then(v.memset(gate, 0.0))
            for t in range(NT):
                then(v.tensor_scalar(gate[:, t, 0:8], sel[:, t, :], gpair[:, 6 + t:7 + t], None, ALU.mult))
                then(v.scalar_tensor_tensor(gate[:, t, 0:8], oh1[:, t, :], gpair[:, 3 + t:4 + t], gate[:, t, 0:8], ALU.mult, ALU.add))
            v.tensor_tensor(sel, sel, oh1, ALU.add).then_inc(sel_ready, 1)
            for t in range(NT):
                dve.wait_ge(*filled(("h2", t, 1)))
                v.tensor_copy(H2[:, t, 512:1024], bank_of(("h2", t, 1))[:, :]).then_inc(drained(("h2", t, 1))[0], 1)
            dve.wait_ge(sel_ready, 1)
            then(v.memset(rank, -1.0))
            dve.wait_ge(*filled("rank"))
            then(v.scalar_tensor_tensor(rank[:, :, 0:8], bank_of("rank")[:, 0:24].rearrange("p (t e) -> p t e", t=NT), 1.0, sel, ALU.add, ALU.mult))
            then(v.tensor_scalar(rank[:, :, 0:8], rank[:, :, 0:8], -1.0, None, ALU.add))
            v.tensor_copy(cnt, bank_of("rank")[:, 24:32]).then_inc(drained("rank")[0], 1)
            dve.wait_ge(*drained("rank"))

            def slots(e, out, gated):
                for t in range(NT):
                    last = v.tensor_scalar(out[:, t, :], iota, rank[:, t, bass.ds(e, 1)] if not isinstance(e, int) else rank[:, t, e:e + 1],
                                           gate[:, t, bass.ds(e, 1)] if gated else None, ALU.is_equal, *([ALU.mult] if gated else []))
                return last

            slots(0, PS, False).then_inc(ps_ready, 1)
            then(v.memset(vsum, 0.0))
            for w_ in WIDTHS[:-1]:
                then(v.scalar_tensor_tensor(vsum[:, 1:9], cnt, float(w_), vsum[:, 1:9], ALU.is_gt, ALU.add))
            then(v.tensor_copy(vtab[:, 0, :], vsum))
            then(v.memset(vsum, 1.0))
            for w_ in (P, 2 * P):
                then(v.scalar_tensor_tensor(vsum[:, 1:9], cnt, float(w_), vsum[:, 1:9], ALU.is_gt, ALU.add))
            v.tensor_copy(vtab[:, 1, :], vsum).then_inc(route_ready, 1)
            dve.wait_ge(moe_zero, 3)
            dve.wait_ge(*filled(("ga0", KT - 1)))

            def moe_bank_of(label):
                return PSUM[place[("moe",) + label][0]]

            with dve.Fori(0, NE) as e:
                slots(e + 1, PS, False).then_inc(ps_ready, 1)
                slots(e, PG, True).then_inc(pg_ready, 1)
                for f in range(FT):
                    dve.wait_ge(*moe_drained(("g", f), e))
                    dve.wait_ge(*moe_filled(("u", f), e))
                    v.tensor_tensor(aT[:, f, :], sg[:, f % 2, :], moe_bank_of(("u", f))[:, 0:TOK], ALU.mult).then_inc(moe_drained(("u", f), e)[0], 1)
                for i in (1, 3, 5):
                    dve.wait_ge(*moe_filled(("T", i), e))
                    v.tensor_copy(yt[:, i // 2, 512:1024], moe_bank_of(("T", i))[:, :]).then_inc(moe_drained(("T", i), e)[0], 1)
                for k in (0, 2):
                    dve.wait_ge(*moe_filled(("dn", k), e))
                    v.tensor_copy(yT[:, k, :], moe_bank_of(("dn", k))[:, 0:TOK]).then_inc(moe_drained(("dn", k), e)[0], 1)
                for i in range(6):
                    dve.wait_ge(*moe_filled(("sc", i), e))
                    ya = YA[:, i // 2, 512 * (i % 2):512 * (i % 2) + 512]
                    v.tensor_tensor(ya, ya, moe_bank_of(("sc", i))[:, :], ALU.add).then_inc(moe_drained(("sc", i), e)[0], 1)
                for k in (4, 6):
                    dve.wait_ge(*moe_filled(("dn", k), e))
                    v.tensor_copy(yT[:, k, :], moe_bank_of(("dn", k))[:, 0:TOK]).then_inc(moe_drained(("dn", k), e)[0], 1)
            for i in (1, 3, 5):
                dve.wait_ge(*filled(("lastT", i)))
                v.tensor_copy(yt[:, i // 2, 512:1024], bank_of(("lastT", i))[:, :]).then_inc(drained(("lastT", i))[0], 1)
            for s in range(2):
                for half in range(2):
                    dve.wait_ge(*drained(("gb", 3, s, half)))
            for i in range(6):
                t, half = i // 2, i % 2
                label = ("last", i)
                dve.wait_ge(*filled(label))
                ya = YA[:, t, 512 * half:512 * half + 512]
                v.tensor_tensor(ya, ya, bank_of(label)[:, :], ALU.add).then_inc(drained(label)[0], 1)
                dve.wait_ge(*drained(label))
                then(v.tensor_tensor(ya, ya, GB[:, 0 if t == 0 else 1, 512 * half:512 * half + 512], ALU.mult))
                x = X[:, t, 512 * half:512 * half + 512]
                v.tensor_tensor(x, x, ya, ALU.add).then_inc(x_updated, 1)

        @block.gpsimd
        def _(pool):
            g_ = nc.gpsimd

            def by_head(a):
                return a.rearrange("p (h d) -> p h d", h=HEADS)

            def over(a):
                return a.unsqueeze(2).broadcast_to([P, HEADS, HD])

            def x_dt(t, d):
                o = 32 * t + 16 * d
                g_.tensor_tensor(by_head(xdt[:, t, d, :]), by_head(XS[:, t, :]), over(dtt[:, o:o + 16]), ALU.mult).then_inc(xdt_ready, 1)

            def x_dt_decay(n, t, d):
                pool.wait_ge(xdt_ready, n)
                o = 32 * t + 16 * d
                g_.tensor_tensor(by_head(W[:, d, :]), by_head(xdt[:, t, d, :]), over(den[:, o:o + 16]), ALU.mult).then_inc(xde_ready, 1)

            pool.wait_ge(dt_ready, 1)
            pool.wait_ge(*filled(("nt", 0, NT - 1, 1)))
            for t in range(NT):
                pool.wait_ge(*drained(("xs", t, 0)))
                pool.wait_ge(*drained(("xs", t, 1)))
            for t, d in ((1, 1), (2, 0), (2, 1)):
                x_dt(t, d)
            pool.wait_ge(ex_ready, 2)
            pool.wait_ge(*filled(("st", 1, 1)))
            pool.wait_ge(*filled((("z", 1, "p"), NT - 1)))
            x_dt(0, 0)
            x_dt_decay(4, 0, 0)
            x_dt(0, 1)
            x_dt_decay(5, 0, 1)
            x_dt(1, 0)
            pool.wait_ge(*filled(("cst", 0, 1)))
            x_dt_decay(6, 1, 0)
            pool.wait_ge(*filled(("cst", 1, 1)))
            x_dt_decay(6, 2, 1)
            for t in range(NT):
                pool.wait_ge(*drained(("cb", t)))
            for i, (t, g) in enumerate(TURNS):
                pool.wait_ge(exp_ready, i + 1)
                w8 = W[:, i % 2, :].rearrange("p (h l) -> p h l", h=8)
                g_.tensor_tensor(w8, w8, cb[:, t, g, :].unsqueeze(1).broadcast_to([P, 8, P]), ALU.mult).then_inc(wm_ready, 1)
            pool.wait_ge(x_updated, 3 * NT)
            g_.memset(yT_a, 0.0).then_inc(moe_zero, 1)
            g_.memset(PGT[:, :, :], 0.0).then_inc(moe_zero, 1)
            g_.memset(YA[:, :, :], 0.0).then_inc(moe_zero, 1)

        @block.sync
        def _(sp):
            def load(n):
                label, parts = chunks[n]
                s = n % RING
                if n >= RING:
                    sp.wait_ge(*released[chunks[n - RING][0]])
                for at, src in parts:
                    k, w = src.shape[1], src.shape[2]
                    sp.dma_start(ring[:, s, at:at + k * w].rearrange("p (k n) -> p k n", k=k), src).then_inc(ring_full[s], 16)

            sp.dma_start(CST[:, :], const_dram).then_inc(const_loaded, 16)
            sp.dma_start(praw[0:8, 0, :], c_ctx.rearrange("(k p) -> k p", p=P)).then_inc(prow_loaded, 16)
            sp.dma_start(praw[8:16, 0, :], c[0].rearrange("(k p) -> k p", p=P)).then_inc(prow_loaded, 16)
            sp.dma_start(praw[16:112, 0, :], b_mod.rearrange("l (m p) -> (l m) p", p=P)).then_inc(prow_loaded, 16)
            sp.dma_start(praw[0:80, 1, :], conv_w[0].rearrange("i (c p) -> (i c) p", p=P)).then_inc(prow_loaded, 16)
            sp.dma_start(praw[80:96, 1, :], conv_b[0].rearrange("(c p) -> c p", p=P)).then_inc(prow_loaded, 16)
            sp.dma_start(praw[96:104, 1, :], ssd_norm[0].rearrange("(c p) -> c p", p=P)).then_inc(prow_loaded, 16)
            sp.dma_start(praw[104:108, 1, :], b_sp[0]).then_inc(prow_loaded, 16)
            sp.dma_start(praw[108:111, 1, :], q_a_norm[0].rearrange("(c p) -> c p", p=P)).then_inc(prow_loaded, 16)
            load(0)
            sp.dma_start(X[:, 0, :], x_prompt[0]).then_inc(x_loaded, 16)
            sp.dma_start(X[:, 1:3, :], x_sample[0].rearrange("(t p) d -> p t d", p=P)).then_inc(x_loaded, 16)
            for n in range(1, RING):
                load(n)
            sp.dma_start(praw[:, 2:6, :], w_sp[0].rearrange("g t s -> t g s")).then_inc(wsp_loaded, 16)
            first_v = [l for l, _ in chunks].index(("v", 0))
            for n in range(RING, first_v):
                load(n)
            sp.wait_ge(*filled("wsp"))
            sp.dma_start(st_raw, state_ssm[0, 0].rearrange("d (i hh) q n -> (hh q) d i n", hh=2)).then_inc(st_loaded, 16)
            first_wout = [l for l, _ in chunks].index(("wout", 2))
            for n in range(first_v, first_wout):
                load(n)
            for d in range(2):
                sp.wait_ge(*drained(("cst", d, 0)))
                sp.wait_ge(*drained(("cst", d, 1)))
                sp.dma_start(new_state[0, 0, d].rearrange("(i hh) q n -> (hh q) i n", hh=2), cst[:, d, :, :]).then_inc(state_out, 16)
            first_dq = [l for l, _ in chunks].index("dq")
            for n in range(first_wout, first_dq):
                load(n)
            sp.wait_ge(x_updated, 2 * NT)
            sp.dma_start(ckv[:, 3, :], cache_ckv[0, 0]).then_inc(cache_loaded, 16)
            sp.dma_start(kpe[:, 3, :], cache_kpe[0, 0]).then_inc(cache_loaded, 16)
            for n in range(first_dq, first_dq + 3):
                load(n)
            sp.wait_ge(ckv_ready, 3)
            sp.dma_start(new_ckv[0, 0], ckv[:, 0, :]).then_inc(kv_out, 16)
            sp.dma_start(new_kpe[0, 0], kpe[:, 0, :]).then_inc(kv_out, 16)
            for n in range(first_dq + 3, STATIC):
                load(n)

            def moe_released(i, e):
                label = MOE_CHUNKS[i]
                if label[1] == "gu":
                    f0, n = GU[label[2]]
                    return moe_filled(("u", f0 + n - 1), e)
                _, _, dp, fh = label
                if fh == 1:
                    return moe_filled(("dn", 2 * dp + 1), e)
                return chunk_used, e * 4 + (used_before_moe[0] + dp + 1)

            def moe_parts(i, e):
                label = MOE_CHUNKS[i]
                if label[1] == "gu":
                    f0, n = GU[label[2]]
                    for at, wgt in ((0, moe_w_gate), (2048, moe_w_up)):
                        yield at, wgt[0, bass.ds(e, 1), :, P * f0:P * (f0 + n)].rearrange("a (k p) n -> p (a k) n", p=P)
                else:
                    _, _, dp, fh = label
                    yield 0, moe_w_down[0, bass.ds(e, 1), FH * P * fh:FH * P * (fh + 1), 256 * dp:256 * dp + 256].rearrange("a (k p) n -> p (a k) n", p=P)

            def moe_load(i, e):
                s = i % RING
                for at, src in moe_parts(i, e):
                    k, w = src.shape[1], src.shape[2]
                    sp.dma_start(ring[:, s, at:at + k * w].rearrange("p (k n) -> p k n", k=k), src).then_inc(ring_full[s], 16)

            for i in range(RING):
                sp.wait_ge(*released[chunks[STATIC - RING + i][0]])
                moe_load(i, 0)
                if i == 0:
                    pass
            sp.wait_ge(x_updated, 3 * NT)
            sp.dma_start(iota, iota_dram).then_inc(iota_loaded, 16)
            with sp.Fori(0, NE - 1) as e:
                for i in range(len(MOE_CHUNKS)):
                    sp.wait_ge(*moe_released(i, e))
                    j = i + RING
                    if MOE_CHUNKS[j % len(MOE_CHUNKS)] == ("moe", "dn", 0, 0):
                        sp.sem_inc(down_begun, 1)
                    moe_load(j % len(MOE_CHUNKS), e + j // len(MOE_CHUNKS))
            for i in range(len(MOE_CHUNKS) - RING):
                sp.wait_ge(*moe_released(i, NE - 1))
                moe_load(i + RING, NE - 1)
            for t in range(NT):
                sp.wait_ge(x_updated, 3 * NT + 2 * (t + 1))
                dst = y_prompt[0] if t == 0 else y_sample[0, (t - 1) * P:t * P, :]
                sp.dma_start(dst, X[:, t, :]).then_inc(y_out, 16)
            sp.wait_ge(state_out, 32)
            sp.wait_ge(kv_out, 32)
            sp.wait_ge(y_out, 48)


_INS = ['x_prompt', 'x_sample', 'c', 'state_ssm', 'cache_ckv', 'cache_kpe', 'c_ctx', 'w_mod', 'b_mod',
        'w_in', 'conv_w', 'conv_b', 'dt_bias', 'a_log', 'd_skip', 'ssd_norm', 'sgu_norm', 'w_sp', 'b_sp', 'w_out',
        'ffn_w_gate', 'ffn_w_up', 'ffn_w_down', 'w_dq', 'q_a_norm', 'w_uq', 'w_dkv', 'kv_a_norm', 'w_ukv',
        'q_norm', 'k_norm', 'w_o', 'router', 'moe_w_gate', 'moe_w_up', 'moe_w_down']
_OUTS = [((1, 128, 1024), 'float32'), ((1, 256, 1024), 'float32'), ((1, 1, 2, 16, 64, 128), 'float32'),
         ((1, 1, 128, 256), 'float32'), ((1, 1, 128, 64), 'float32')]


def kernel(**inputs):
    import numpy as _np
    import concourse.bacc as _bacc
    from concourse import mybir as _mybir
    from concourse.bass_utils import run_bass_kernel_spmd as _run

    nc = _bacc.Bacc("TRN2", target_bir_lowering=False, num_devices=1, dynamic_dma_scratch_size=1024)
    arrays, args = {}, []
    for name in _INS:
        a = _np.ascontiguousarray(inputs[name])
        arrays[f"in_{name}_dram"] = a
        args.append(nc.dram_tensor(f"in_{name}_dram", a.shape, _mybir.dt.from_np(a.dtype), kind="ExternalInput").ap())
    for i, (shape, dtype) in enumerate(_OUTS):
        dt = _mybir.dt.from_np(_np.dtype(dtype))
        args.append(nc.dram_tensor(f"out_{i}_dram", shape, dt, kind="ExternalOutput").ap())
    hybrid_trunk(nc, *args)
    r = _run(nc, [arrays], core_ids=[0])
    return tuple(r.results[0][f"out_{i}_dram"] for i in range(len(_OUTS)))
```
